# Optimizing a Trainium2 kernel written in Bass

```python
import jax, jax.numpy as jnp
from jax import lax
import numpy as np

D_MODEL = 1024
BATCH = 1
SEQ = 128
DEPTH = 2
DEC_BATCH = 1
DEC_SEQ = 256
PAST_LEN = 128

GRID_W = 64
EPS = 1e-6
CONV_CH = 512
CONV_WIDTH = 31
N_Q_HEADS = 8
N_KV_HEADS = 2
Q_PER_KV = N_Q_HEADS // N_KV_HEADS
HEAD_DIM = 128
Q_BLOCK = 128
ROPE_THETA = 10000.0
ATTN_WIDTH = N_Q_HEADS * HEAD_DIM
KV_WIDTH = N_KV_HEADS * HEAD_DIM
IN0_WIDTH = 2 * CONV_CH + ATTN_WIDTH + 2 * KV_WIDTH
OUT0_WIDTH = CONV_CH + ATTN_WIDTH
SPLIT0 = [CONV_CH, 2 * CONV_CH, 2 * CONV_CH + ATTN_WIDTH, 2 * CONV_CH + ATTN_WIDTH + KV_WIDTH]
RET_HEADS = 8
RET_DK = 128
RET_DV = 256
RET_CHUNK = 128
RET_QK_WIDTH = RET_HEADS * RET_DK
RET_V_WIDTH = RET_HEADS * RET_DV
IN1_WIDTH = 2 * RET_QK_WIDTH + 3 * RET_V_WIDTH
SPLIT1 = [RET_QK_WIDTH, 2 * RET_QK_WIDTH, 2 * RET_QK_WIDTH + RET_V_WIDTH, 2 * RET_QK_WIDTH + 2 * RET_V_WIDTH]
N_GROUPS = 4
EXPERTS_PER_GROUP = 4
N_EXPERTS = N_GROUPS * EXPERTS_PER_GROUP
EXPERT_FF = 512
TOP_K = 2

kernel_name = 'hybrid_diffusion_conv_gqa_retention_hmoe_step'

def rmsnorm(x, g):
    xf = x.astype(jnp.float32)
    y = xf * lax.rsqrt(jnp.mean(xf * xf, axis=-1, keepdims=True) + EPS)
    return (y * g.astype(jnp.float32)).astype(x.dtype)

def layernorm(x, g, b):
    xf = x.astype(jnp.float32)
    mu = jnp.mean(xf, axis=-1, keepdims=True)
    var = jnp.mean(jnp.square(xf - mu), axis=-1, keepdims=True)
    y = (xf - mu) * lax.rsqrt(var + EPS)
    return (y * g.astype(jnp.float32) + b.astype(jnp.float32)).astype(x.dtype)

def grid_rope_tables(n_tokens, dim):
    rows = n_tokens // GRID_W
    t = jnp.arange(rows * GRID_W)
    pos = jnp.stack([t // GRID_W, t % GRID_W]).astype(jnp.float32)
    n_freq = dim // 4
    freqs = ROPE_THETA ** (-jnp.arange(n_freq, dtype=jnp.float32) / n_freq)
    ang = pos[:, :, None] * freqs
    return jnp.cos(ang), jnp.sin(ang)

def apply_grid_rope(x, cos, sin):
    dim = x.shape[-1]
    half, quarter = dim // 2, dim // 4
    xf = x.astype(jnp.float32)

    def rot(xa, c, s):
        x1, x2 = xa[..., :quarter], xa[..., quarter:]
        return jnp.concatenate([x1 * c - x2 * s, x1 * s + x2 * c], axis=-1)

    out = jnp.concatenate([rot(xf[..., :half], cos[0], sin[0]), rot(xf[..., half:], cos[1], sin[1])], axis=-1)
    return out.astype(x.dtype)

def block_attention(q, k, v):
    B, H, G, T, hd = q.shape
    nb = T // Q_BLOCK
    kf, vf = k.astype(jnp.float32), v.astype(jnp.float32)
    qb = jnp.moveaxis(q.reshape(B, H, G, nb, Q_BLOCK, hd), 3, 0)
    scale = hd ** -0.5

    def attend(qi):
        s = jnp.einsum('bhgqd,bhkd->bhgqk', qi.astype(jnp.float32), kf) * scale
        p = jax.nn.softmax(s, axis=-1)
        return jnp.einsum('bhgqk,bhkd->bhgqd', p, vf)

    o = lax.map(attend, qb)
    return jnp.moveaxis(o, 0, 3).reshape(B, H, G, T, hd).astype(q.dtype)

def mix_attn_conv(h, rope, ctx_kv, in_w, conv_w, conv_b, conv_norm_g, conv_norm_b, q_norm_g, k_norm_g, out_w):
    B, T, _ = h.shape
    a_val, a_gate, q, k, v = jnp.split(h @ in_w, SPLIT0, axis=-1)
    a = a_val * jax.nn.sigmoid(a_gate)
    a = lax.conv_general_dilated(a, conv_w[:, None, :], (1,), [(CONV_WIDTH // 2, CONV_WIDTH // 2)],
                                 dimension_numbers=('NWC', 'WIO', 'NWC'), feature_group_count=CONV_CH) + conv_b
    a = jax.nn.silu(layernorm(a, conv_norm_g, conv_norm_b))
    q = rmsnorm(q.reshape(B, T, N_Q_HEADS, HEAD_DIM), q_norm_g).transpose(0, 2, 1, 3)
    k = rmsnorm(k.reshape(B, T, N_KV_HEADS, HEAD_DIM), k_norm_g).transpose(0, 2, 1, 3)
    v = v.reshape(B, T, N_KV_HEADS, HEAD_DIM).transpose(0, 2, 1, 3)
    if rope is not None:
        q = apply_grid_rope(q, *rope)
        k = apply_grid_rope(k, *rope)
    keys, vals = k, v
    if ctx_kv is not None:
        keys = jnp.concatenate([ctx_kv[0].astype(k.dtype), k], axis=2)
        vals = jnp.concatenate([ctx_kv[1].astype(v.dtype), v], axis=2)
    o = block_attention(q.reshape(B, N_KV_HEADS, Q_PER_KV, T, HEAD_DIM), keys, vals)
    o = o.reshape(B, N_Q_HEADS, T, HEAD_DIM).transpose(0, 2, 1, 3).reshape(B, T, ATTN_WIDTH)
    return jnp.concatenate([a, o], axis=-1) @ out_w, (k, v)

def retention_chunkwise(q, k, v, log_gamma, state0):
    B, H, T, dk = q.shape
    dv = v.shape[-1]
    C = RET_CHUNK
    n = T // C
    f32 = jnp.float32
    qc = jnp.moveaxis(q.astype(f32).reshape(B, H, n, C, dk), 2, 0)
    kc = jnp.moveaxis(k.astype(f32).reshape(B, H, n, C, dk), 2, 0)
    vc = jnp.moveaxis(v.astype(f32).reshape(B, H, n, C, dv), 2, 0)
    pos = jnp.arange(C, dtype=f32)
    diff = pos[:, None] - pos[None, :]
    lg = log_gamma.astype(f32)[:, None, None]
    intra = jnp.where(diff >= 0, jnp.exp(lg * jnp.maximum(diff, 0.0)), 0.0)
    q_dec = jnp.exp(lg[:, :, 0] * (pos + 1.0))[:, :, None]
    k_dec = jnp.exp(lg[:, :, 0] * (C - 1.0 - pos))[:, :, None]
    chunk_dec = jnp.exp(lg * C)

    def step(S, blk):
        qi, ki, vi = blk
        s = jnp.einsum('bhqd,bhkd->bhqk', qi, ki) * intra
        y = jnp.einsum('bhqk,bhke->bhqe', s, vi) + jnp.einsum('bhqd,bhde->bhqe', qi, S) * q_dec
        S = S * chunk_dec + jnp.einsum('bhkd,bhke->bhde', ki * k_dec, vi)
        return S, y

    S, y = lax.scan(step, state0.astype(f32), (qc, kc, vc))
    return jnp.moveaxis(y, 0, 2).reshape(B, H, T, dv), S

def head_rms(y):
    y = y * lax.rsqrt(jnp.mean(y * y, axis=-1, keepdims=True) + EPS)
    B, H, T, dv = y.shape
    return y.transpose(0, 2, 1, 3).reshape(B, T, H * dv)

def mix_retention(h, rope, states, in_w, decay_fwd, decay_bwd, out_w):
    B, T, _ = h.shape
    q, k, v, g_f, g_b = jnp.split(h @ in_w, SPLIT1, axis=-1)
    q = q.reshape(B, T, RET_HEADS, RET_DK).transpose(0, 2, 1, 3)
    k = k.reshape(B, T, RET_HEADS, RET_DK).transpose(0, 2, 1, 3)
    v = v.reshape(B, T, RET_HEADS, RET_DV).transpose(0, 2, 1, 3)
    if rope is not None:
        q = apply_grid_rope(q, *rope)
        k = apply_grid_rope(k, *rope)
    k = k * (RET_DK ** -0.5)
    log_gamma_f = -jnp.exp(decay_fwd.astype(jnp.float32))
    log_gamma_b = -jnp.exp(decay_bwd.astype(jnp.float32))
    if states is None:
        s0_f = jnp.zeros((B, RET_HEADS, RET_DK, RET_DV), jnp.float32)
        s0_b = s0_f
    else:
        s0_f, s0_b = states
    y_f, s_f = retention_chunkwise(q, k, v, log_gamma_f, s0_f)
    y_b, s_b = retention_chunkwise(jnp.flip(q, 2), jnp.flip(k, 2), jnp.flip(v, 2), log_gamma_b, s0_b)
    y_b = jnp.flip(y_b, 2)
    mixed = (jax.nn.silu(g_f.astype(jnp.float32)) * head_rms(y_f)
             + jax.nn.silu(g_b.astype(jnp.float32)) * head_rms(y_b))
    return mixed.astype(h.dtype) @ out_w, (s_f, s_b)

def hier_moe(h, grp_w, grp_b, rtr_w, rtr_b, w_gate, w_up, w_down):
    B, T, D = h.shape
    x = h.reshape(B * T, D)
    g_logits = (x @ grp_w + grp_b).astype(jnp.float32)
    g_prob = jax.nn.softmax(g_logits, axis=-1)
    g_idx = jnp.argmax(g_logits, axis=-1)
    g_w = jnp.take_along_axis(g_prob, g_idx[:, None], axis=-1)
    e_all = (jnp.einsum('nd,gde->nge', x, rtr_w) + rtr_b).astype(jnp.float32)
    e_logits = jnp.take_along_axis(e_all, g_idx[:, None, None], axis=1)[:, 0]
    top_v, top_i = lax.top_k(e_logits, TOP_K)
    top_w = jax.nn.softmax(top_v, axis=-1) * g_w
    expert_id = g_idx[:, None] * EXPERTS_PER_GROUP + top_i
    combine = jnp.sum(jax.nn.one_hot(expert_id, N_EXPERTS, dtype=jnp.float32) * top_w[..., None], axis=1)
    hidden = jax.nn.silu(jnp.einsum('nd,edf->nef', x, w_gate)) * jnp.einsum('nd,edf->nef', x, w_up)
    y = jnp.einsum('nef,efd->nd', hidden * combine[:, :, None].astype(hidden.dtype), w_down)
    return y.reshape(B, T, D)

def trunk_layer(x, cond, mod_w, mod_b, norm_mix_g, norm_ffn_g, moe_params, mixer_fn):
    mod = (jax.nn.silu(cond) @ mod_w + mod_b).reshape(cond.shape[0], 6, D_MODEL)
    shift_m, scale_m, gate_m, shift_f, scale_f, gate_f = [mod[:, i, None, :] for i in range(6)]
    h = rmsnorm(x, norm_mix_g) * (1.0 + scale_m) + shift_m
    out, ctx_tensors = mixer_fn(h)
    x = x + gate_m * out
    h = rmsnorm(x, norm_ffn_g) * (1.0 + scale_f) + shift_f
    x = x + gate_f * hier_moe(h, *moe_params)
    return x, ctx_tensors

def setup_inputs(seed: int = 0) -> dict:
    key = jax.random.key(seed)
    ks = iter(jax.random.split(key, 80))

    def nrm(shape, scale):
        return scale * jax.random.normal(next(ks), shape, jnp.float32)

    D = D_MODEL
    inp = {}
    inp['x_prompt'] = nrm((BATCH, SEQ, D), 1.0)
    inp['x_sample'] = nrm((DEC_BATCH, DEC_SEQ, D), 1.0)
    inp['cache_k0'] = nrm((DEC_BATCH, N_KV_HEADS, PAST_LEN, HEAD_DIM), 1.0)
    inp['cache_v0'] = nrm((DEC_BATCH, N_KV_HEADS, PAST_LEN, HEAD_DIM), 1.0)
    inp['state_ret_fwd1'] = nrm((DEC_BATCH, RET_HEADS, RET_DK, RET_DV), 0.1)
    inp['state_ret_bwd1'] = nrm((DEC_BATCH, RET_HEADS, RET_DK, RET_DV), 0.1)
    inp['c'] = nrm((DEC_BATCH, D), 1.0)
    inp['c_ctx'] = nrm((D,), 1.0)

    def moe(i):
        inp['moe_grp_w%d' % i] = nrm((D, N_GROUPS), D ** -0.5)
        inp['moe_grp_b%d' % i] = nrm((N_GROUPS,), 0.01)
        inp['moe_rtr_w%d' % i] = nrm((N_GROUPS, D, EXPERTS_PER_GROUP), D ** -0.5)
        inp['moe_rtr_b%d' % i] = nrm((N_GROUPS, EXPERTS_PER_GROUP), 0.01)
        inp['moe_w_gate%d' % i] = nrm((N_EXPERTS, D, EXPERT_FF), D ** -0.5)
        inp['moe_w_up%d' % i] = nrm((N_EXPERTS, D, EXPERT_FF), D ** -0.5)
        inp['moe_w_down%d' % i] = nrm((N_EXPERTS, EXPERT_FF, D), EXPERT_FF ** -0.5)

    inp['norm_mix_g0'] = 1.0 + nrm((D,), 0.05)
    inp['mod_w0'] = nrm((D, 6 * D), 0.5 * D ** -0.5)
    inp['mod_b0'] = nrm((6 * D,), 0.02)
    inp['in_w0'] = nrm((D, IN0_WIDTH), D ** -0.5)
    inp['conv_w0'] = nrm((CONV_WIDTH, CONV_CH), CONV_WIDTH ** -0.5)
    inp['conv_b0'] = nrm((CONV_CH,), 0.02)
    inp['conv_norm_g0'] = 1.0 + nrm((CONV_CH,), 0.05)
    inp['conv_norm_b0'] = nrm((CONV_CH,), 0.02)
    inp['q_norm_g0'] = 1.0 + nrm((HEAD_DIM,), 0.05)
    inp['k_norm_g0'] = 1.0 + nrm((HEAD_DIM,), 0.05)
    inp['out_w0'] = nrm((OUT0_WIDTH, D), OUT0_WIDTH ** -0.5)
    inp['norm_ffn_g0'] = 1.0 + nrm((D,), 0.05)
    moe(0)
    inp['norm_mix_g1'] = 1.0 + nrm((D,), 0.05)
    inp['mod_w1'] = nrm((D, 6 * D), 0.5 * D ** -0.5)
    inp['mod_b1'] = nrm((6 * D,), 0.02)
    inp['in_w1'] = nrm((D, IN1_WIDTH), D ** -0.5)
    base = jnp.log(-jnp.log1p(-(2.0 ** (-5.0 - jnp.arange(RET_HEADS, dtype=jnp.float32)))))
    inp['ret_decay_fwd1'] = base + nrm((RET_HEADS,), 0.05)
    inp['ret_decay_bwd1'] = base + nrm((RET_HEADS,), 0.05)
    inp['out_w1'] = nrm((RET_V_WIDTH, D), RET_V_WIDTH ** -0.5)
    inp['norm_ffn_g1'] = 1.0 + nrm((D,), 0.05)
    moe(1)
    inp['final_norm_g'] = 1.0 + nrm((D,), 0.05)
    return inp

def reference(x_prompt, x_sample, cache_k0, cache_v0, state_ret_fwd1, state_ret_bwd1, c, c_ctx,
              norm_mix_g0, mod_w0, mod_b0, in_w0, conv_w0, conv_b0, conv_norm_g0, conv_norm_b0,
              q_norm_g0, k_norm_g0, out_w0, norm_ffn_g0,
              moe_grp_w0, moe_grp_b0, moe_rtr_w0, moe_rtr_b0, moe_w_gate0, moe_w_up0, moe_w_down0,
              norm_mix_g1, mod_w1, mod_b1, in_w1, ret_decay_fwd1, ret_decay_bwd1, out_w1, norm_ffn_g1,
              moe_grp_w1, moe_grp_b1, moe_rtr_w1, moe_rtr_b1, moe_w_gate1, moe_w_up1, moe_w_down1,
              final_norm_g):
    n_lat = x_sample.shape[1]
    rope_attn = grid_rope_tables(n_lat, HEAD_DIM)
    rope_ret = grid_rope_tables(n_lat, RET_DK)
    layers = [
        dict(mod=(mod_w0, mod_b0), norms=(norm_mix_g0, norm_ffn_g0), mixer_fn=mix_attn_conv, rope=rope_attn,
             mixer=(in_w0, conv_w0, conv_b0, conv_norm_g0, conv_norm_b0, q_norm_g0, k_norm_g0, out_w0),
             moe=(moe_grp_w0, moe_grp_b0, moe_rtr_w0, moe_rtr_b0, moe_w_gate0, moe_w_up0, moe_w_down0),
             cache=(cache_k0, cache_v0)),
        dict(mod=(mod_w1, mod_b1), norms=(norm_mix_g1, norm_ffn_g1), mixer_fn=mix_retention, rope=rope_ret,
             mixer=(in_w1, ret_decay_fwd1, ret_decay_bwd1, out_w1),
             moe=(moe_grp_w1, moe_grp_b1, moe_rtr_w1, moe_rtr_b1, moe_w_gate1, moe_w_up1, moe_w_down1),
             cache=(state_ret_fwd1, state_ret_bwd1)),
    ]
    xp, xs = x_prompt, x_sample
    new_state = []
    for layer in range(DEPTH):
        p = layers[layer]
        mixer_fn, rope, mparams, cache = p['mixer_fn'], p['rope'], p['mixer'], p['cache']
        xp, ctx_tensors = trunk_layer(xp, c_ctx[None, :], p['mod'][0], p['mod'][1], p['norms'][0], p['norms'][1],
                                      p['moe'], lambda h: mixer_fn(h, None, None, *mparams))
        new_state.extend(ctx_tensors)
        xs, _ = trunk_layer(xs, c, p['mod'][0], p['mod'][1], p['norms'][0], p['norms'][1],
                            p['moe'], lambda h: mixer_fn(h, rope, cache, *mparams))
    y_prompt = rmsnorm(xp, final_norm_g)
    y_sample = rmsnorm(xs, final_norm_g)
    new_k0, new_v0, new_state_ret_fwd1, new_state_ret_bwd1 = new_state
    return (y_prompt, y_sample, new_k0, new_v0, new_state_ret_fwd1, new_state_ret_bwd1)


_drawn_inputs = setup_inputs


def setup_inputs(seed=0):
    import zlib

    import numpy as np

    out = dict(_drawn_inputs(seed))
    spreads = {}
    factors = {'cache_k0': 4.251,
     'cache_v0': 3.805,
     'conv_b0': 4.79,
     'conv_norm_g0': 4.287,
     'conv_norm_b0': 8.0,
     'q_norm_g0': 8.0,
     'norm_ffn_g0': 3.02,
     'moe_grp_b0': 8.0,
     'moe_rtr_b0': 8.0,
     'norm_ffn_g1': 3.443,
     'moe_grp_b1': 8.0,
     'moe_rtr_b1': 8.0}
    for name, (base, spread) in spreads.items():
        noise = np.random.default_rng([zlib.crc32(name.encode()), seed]).standard_normal(out[name].shape)
        drawn = base * np.exp(spread * noise) if base else spread * noise
        out[name] = __import__('jax').numpy.asarray(drawn.astype(out[name].dtype))
    for name, factor in factors.items():
        out[name] = (out[name] * factor).astype(out[name].dtype)
    return out
```

```python
from contextlib import ExitStack

import numpy as np

import concourse.bass as bass
from concourse import mybir

F32 = mybir.dt.float32
I32 = mybir.dt.int32
ALU = mybir.AluOpType
ACT = mybir.ActivationFunctionType
AX = mybir.AxisListType.X

P = 128
D = 1024
KD = D // P
TT = 3
NT = TT * P
SLOT = 4096
NSLOT = 6
CONV = 512
CB = CONV // P
TAPS = 31
PAD = TAPS // 2
CTX0 = PAD
LAT0 = PAD + P + PAD + PAD
APAD = LAT0 + 2 * P + PAD
CVN = APAD - 2 * PAD
TOKCOL = [CTX0 - PAD, LAT0 - PAD, LAT0 - PAD + P]
QH, KH, HD = 8, 2, 128
HQK = QH + KH
QPK = QH // KH
RH, DK, DV = 8, 128, 256
NG, EG, NE = 4, 4, 16
PAIRS = NE // 2
FF = 512
CAP = 64
UNITS = NT // CAP
EPS = 1e-6
BIG = 1e30

C_ID, C_ONE, C_IOTA, C_UPPER = 0, 128, 256, 320
C_DF, C_DB, C_MF, C_MB = 448, 576, 704, 832
C_COS, C_SIN = 960, 1216
C_SEL2, C_IOTA4, C_POS, C_EPS = 1472, 1474, 1478, 1482
C_ALL = 1484
V_MODB, V_NG, V_CB, V_CNG, V_CNB, V_CW, V_COND = 0, 96, 128, 132, 136, 140, 264
V_RW, V_RB, V_DEC, V_QKG = 280, 600, 640, 656
V_ALL = 912

STEP_COL = {"q": 0, "k": RH * DK, "v": 2 * RH * DK, "f": 2 * RH * DK + RH * DV, "b": 2 * RH * DK + 2 * RH * DV}


def plan_retention():
    def jobs(*steps):
        return [("job", s, t) for s in steps for t in range(TT)]

    def outs(j, a, b):
        return [("out", j, i) for i in range(a, b)]

    e = jobs("q0", "k0") + [("gate", 0, 0)] + jobs("v0") + [("turn", 0, 0)] + jobs("f0", "b0")
    f = jobs("v1", "f1", "b1")
    e += [("A", 0, 0)] + f[0:2] + [("B", 0, 0)] + f[2:4] + [("A", 1, 0)] + f[4:6] + [("C", 0, 0)] + f[6:7]
    e += [("B", 1, 0)] + f[7:9]
    f = jobs("v2", "f2", "b2")
    e += [("A", 2, 0)] + [("C", 1, 0)] + outs(0, 0, 6) + [("B", 2, 0)] + f[0:2] + [("A", 3, 0)] + f[2:4]
    e += [("C", 2, 0)] + f[4:5] + [("B", 3, 0)] + f[5:9] + [("C", 3, 0)]
    e += jobs("q1", "k1") + outs(1, 0, 6) + [("turn", 1, 0)]
    f = jobs("v3", "f3", "b3")
    e += f[0:1] + [("A", 4, 0)] + f[1:3] + [("B", 4, 0)] + f[3:5] + [("A", 5, 0)] + f[5:7] + [("C", 4, 0)] + f[7:8]
    e += [("B", 5, 0)] + f[8:9]
    e += [("A", 6, 0), ("C", 5, 0)] + outs(2, 0, 4) + [("B", 6, 0)] + outs(2, 4, 6)
    e += [("A", 7, 0), ("C", 6, 0), ("B", 7, 0), ("C", 7, 0)] + outs(3, 0, 6)
    return e


RET = plan_retention()

STREAM, PLACE = [], []


def plan_stream():
    def put(kind, layer, chunks, slots):
        for i, c in enumerate(chunks):
            STREAM.append((kind, layer, c))
            PLACE.append(slots[i % len(slots)])

    put("mod", 0, range(12), [0, 1, 2, 3, 4])
    put("in", 0, range(5), [2, 3, 4, 0, 1])
    put("mod", 1, range(12), [2, 3, 4, 0, 1])
    put("out", 0, [1, 2, 0], [4, 0, 1])
    put("moe", 0, range(6 * PAIRS), range(6))
    seen = []
    for kind, step, _ in RET:
        key = ("in", 1, step) if kind == "job" else ("out", 1, step) if kind == "out" else None
        if key and key not in seen:
            seen.append(key)
    for n, (kind, layer, c) in enumerate(seen):
        put(kind, layer, [c], [n % 4])
    put("moe", 1, range(6 * PAIRS), range(6))


plan_stream()
INDEX = {key: i for i, key in enumerate(STREAM)}
USES = [sum(PLACE[j] == PLACE[i] for j in range(i)) for i in range(len(STREAM))]
BEFORE = [max([j for j in range(i) if PLACE[j] == PLACE[i]], default=None) for i in range(len(STREAM))]

JOBS = {}
for _c, _k in ((0, CB), (1, CB), (2, TT), (3, TT), (4, TT)):
    for _t in range(_k):
        JOBS[(0, _c, _t)] = len(JOBS) + 1
for _kind, _s, _t in RET:
    if _kind == "job":
        JOBS[(1, _s, _t)] = len(JOBS) + 1
JOBS0 = 2 * CB + 3 * TT
MOD_BANK, MOD_COLS = (6, 1), (5, 0)
SHARED = [e for e in RET if e[0] in ("job", "out")]
ROPES = [e for e in SHARED if e[0] == "job" and e[1][0] in "qk" and e[2] > 0]
UNTIL = {e: n for n, e in enumerate(SHARED)}
COPY_NO = {e: n + 1 for n, e in enumerate([e for e in SHARED if e[0] == "job"])}
OUT_NO = {e: n + 1 for n, e in enumerate([e for e in SHARED if e[0] == "out"])}
ROPE_NO = {e: n + 1 for n, e in enumerate(ROPES)}
ROPED = {e: sum(r in RET[:RET.index(e)] for r in ROPES) for e in SHARED}


def backbone_kernel(nc, x_in, cst, par, fgain, cache_k, cache_v, st_in, mod_w, in_w, out_w, w_gate,
                    w_up, w_down, y_out, new_k, new_v, st_out):
    with ExitStack() as ctx:
        def sb(name, shape, dt=F32):
            return ctx.enter_context(nc.sbuf_tensor(name, shape, dt))[:]

        def sem(name):
            return ctx.enter_context(nc.semaphore(name))

        PS = ctx.enter_context(nc.psum_tensor("PS", [P, 8, 512], F32))

        ring = sb("ring", [P, NSLOT * SLOT])
        x = sb("x", [P, TT, D])
        hT = sb("hT", [P, KD, NT])
        gate_row = sb("gate_row", [P, 2, D])
        C = sb("C", [P, C_ALL])
        V = sb("V", [P, V_ALL])
        cond = sb("cond", [P, KD, 32])
        modc = sb("modc", [P, 2, 48, 2])
        gain = sb("gain", [P, 4, KD, 2])
        stat = sb("stat", [P, 64])
        counts = sb("counts", [P, PAIRS], I32)
        AREA = 17400
        area = sb("area", [P, AREA])

        ident, ones = C[:, C_ID:C_ID + P], C[:, C_ONE:C_ONE + P]
        eps = C[:, C_EPS:C_EPS + 1]
        iota_cap = C[:, C_IOTA:C_IOTA + CAP]
        iota4 = C[:, C_IOTA4:C_IOTA4 + 4]
        junk = gate_row[:, 0, :]

        def slot(i):
            return ring[:, i * SLOT:(i + 1) * SLOT]

        def cutter(*areas):
            left = [[a, 0, n] for a, n in areas]

            def take(*shape):
                n = int(np.prod(shape))
                a = next(a for a in left if a[1] + n <= a[2])
                v = a[0][:, a[1]:a[1] + n]
                a[1] += n
                if len(shape) == 1:
                    return v
                names = "abcd"[:len(shape)]
                return v.rearrange(f"p ({' '.join(names)}) -> p {' '.join(names)}", **dict(zip(names, shape)))
            return take

        m = cutter((area, AREA))
        h, acc, diag_f = m(TT, D), m(TT, D), m(2, KD, P)
        xn = h
        sel, selw, selT, selT_ov = m(TT, P), m(TT, P), m(TT, P), m(TT, P)
        gT, gT_ov = m(KD, P), m(KD, P)
        sgate, hid, hidT = m(FF), m(FF), m(4, P)
        ysb, y_ov = m(D), m(D)
        fg = m(D)
        lg = m(TT, 20)
        gd, ge, cd, oh, es, es2, o1, o2, ed = (m(TT, 4) for _ in range(9))
        em, mem, comb, key = m(TT, 16), m(TT, 16), m(TT, 16), m(TT, 16)
        rs = m(10, TT)
        cntf = m(PAIRS)
        kA, kB, cB = m(TT, 2), m(TT, 2), m(TT, 2)

        a0 = cutter((area, AREA))
        qk = a0(TT, HQK, HD)
        vv = a0(4, KH, HD)
        kT = a0(KH, 4, P)
        kc = a0(KH, HD)
        cv, apad, tmp2 = a0(CB, CVN), a0(CB, APAD), a0(2, HQK, HD)
        qT, modrow, ctap = a0(QH, NT), a0(2, 512), a0(2, CVN)
        oT = slot(5)[:, 0:QH * NT].rearrange("p (a b) -> p a b", a=QH)
        diag_0 = qT.rearrange("p a b -> p (a b)")[:, 0:2 * D].rearrange("p (c k j) -> p c k j", c=2, k=KD)
        tm = tmp2.rearrange("p a b c -> p (a b c)")
        sig = tm[:, 0:CB * NT].rearrange("p (a b) -> p a b", a=CB)
        pr = tm[:, 0:2 * NT].rearrange("p (a b) -> p a b", a=2)
        prT = tm[:, 2 * NT:4 * NT].rearrange("p (a b) -> p a b", a=2)
        z = qk.rearrange("p a b c -> p (a b c)")[:, 0:TT * CONV].rearrange("p (a b) -> p a b", a=TT)
        aT = apad.rearrange("p a b -> p (a b)")[:, 0:CB * NT].rearrange("p (a b) -> p a b", a=CB)

        a1 = cutter((area, AREA), (ring[:, 4 * SLOT:6 * SLOT], 2 * SLOT))
        q1T, k1T = a1(4, NT), a1(4, NT)
        ktok, yr, mixT = a1(TT, 512), a1(TT, 2, DV), a1(4, NT)
        qtok = yr.rearrange("p a b c -> p a (b c)")
        masks, kd, smask, mix = a1(RH, 2, P), a1(4, P), a1(2, TT, P), a1(TT, DV)
        smask_v = smask.rearrange("p a b c -> p (a b c)").rearrange("p (a b) -> p a b", a=TT)
        st0, st1, stout, rtmp = a1(2, 2, DV), a1(2, DV), a1(2, DV), a1(2, 512)
        dec = a1(5, 2 * RH)
        v1 = [a1(TT, 512)]
        v1.append(a1(TT, 512))
        sg1 = [a1(2, TT, 512), a1(2, TT, 512)]
        diag_1 = sg1[1].rearrange("p a b c -> p (a b c)")[:, 0:2 * D].rearrange("p (c k j) -> p c k j", c=2, k=KD)
        diags = [diag_0, diag_f, diag_1, diag_f]

        par_loaded, x_loaded, cache_loaded = sem("par_loaded"), [sem(f"x_loaded{t}") for t in range(TT)], sem("cache_loaded")
        ring_loaded = [sem(f"ring_loaded{i}") for i in range(NSLOT)]
        cond_ready, mod_mm, mod_copied, mod_col_mm, mod_ready, gain_ready = map(sem, (
            "cond_ready", "mod_mm", "mod_copied", "mod_col_mm", "mod_ready", "gain_ready"))
        sumsq, rms, xn_ready, xnT_mm, hT_dve, hT_act, x_ready = map(sem, (
            "sumsq", "rms", "xn_ready", "xnT_mm", "hT_dve", "hT_act", "x_ready"))
        diag_ready, gate_mm, gate_copied, proj_mm, out_slot, out_mm, out_add = map(sem, (
            "diag_ready", "gate_mm", "gate_copied", "proj_mm", "out_slot", "out_mm", "out_add"))
        sig_done, glu_done, qk_copied, qk_sq, qk_rms, qk_ready, qkT_mm, qkT_act, qkT_dve = map(sem, (
            "sig_done", "glu_done", "qk_copied", "qk_sq", "qk_rms", "qk_ready", "qkT_mm", "qkT_act", "qkT_dve"))
        s_mm, s_max, exp_done, pr_ready, prT_mm, prT_copied, o_mm, o_copied, kv_out = map(sem, (
            "s_mm", "s_max", "exp_done", "pr_ready", "prT_mm", "prT_copied", "o_mm", "o_copied", "kv_out"))
        pad_zero, conv_pool, conv_dve, ln_mm, ln_var, ln_std, z_ready, zT_mm, aT_ready = map(sem, (
            "pad_zero", "conv_pool", "conv_dve", "ln_mm", "ln_var", "ln_std", "z_ready", "zT_mm", "aT_ready"))
        router_mm, route_d, route_e, mem_ready, rank_mm, counts_ready, hback_mm, h_copied = map(sem, (
            "router_mm", "route_d", "route_e", "mem_ready", "rank_mm", "counts_ready", "hback_mm", "h_copied"))
        pairkey, sel_ready, selw_ready, gath_mm, gath_copied, egate_mm, eup_mm, silu_done, hid_ready = map(sem, (
            "pairkey", "sel_ready", "selw_ready", "gath_mm", "gath_copied", "egate_mm", "eup_mm", "silu_done", "hid_ready"))
        hidT_mm, hidT_copied, selT_mm, selT_copied, down_mm, y_copied, scat_mm, acc_add, = map(sem, (
            "hidT_mm", "hidT_copied", "selT_mm", "selT_copied", "down_mm", "y_copied", "scat_mm", "acc_add"))
        expert_free = [sem("gate_free"), sem("up_free"), sem("down_free")]
        ov_pe, ov_act, ov_dve = sem("ov_pe"), sem("ov_act"), sem("ov_dve")
        dec_ready, mask_exp, mask_ready, job_copied, rope_done, turn_mm, turn_copied = map(sem, (
            "dec_ready", "mask_exp", "mask_ready", "job_copied", "rope_done", "turn_mm", "turn_copied"))
        kd_ready, rA_mm, smask_ready, st1_ready, rB_mm, yr_ready, yr_sq, yr_rms, mix_ready = map(sem, (
            "kd_ready", "rA_mm", "smask_ready", "st1_ready", "rB_mm", "yr_ready", "yr_sq", "yr_rms", "mix_ready"))
        mixT_mm, mixT_copied, stout_ready, state_out = map(sem, ("mixT_mm", "mixT_copied", "stout_ready", "state_out"))
        st_loaded = [sem("st_loaded0"), sem("st_loaded1")]
        y_ready, y_stored, fg_loaded = sem("y_ready"), sem("y_stored"), sem("fg_loaded")
        dve_chain, pool_chain = sem("dve_chain"), sem("pool_chain")

        def need(eng, s, value):
            if not isinstance(value, int) or value > 0:
                eng.wait_ge(s, value)

        def cols(t):
            return slice(t * P, (t + 1) * P)

        def cnd(t):
            return 0 if t == 0 else 1

        def arrived(eng, i):
            eng.wait_ge(ring_loaded[PLACE[i]], 16 * (USES[i] + 1))

        def wslot(i):
            kind, _, c = STREAM[i]
            wide = kind == "out" or (kind == "moe" and c % 6 >= 4)
            return slot(PLACE[i]).rearrange("p (k n) -> p k n", n=D if wide else 512)

        def released(eng, i):
            kind, l, c = STREAM[i]
            if kind == "mod":
                eng.wait_ge(mod_mm, 12 * l + c + 1)
            elif kind == "in":
                eng.wait_ge(proj_mm, JOBS[(l, c, CB - 1 if l == 0 and c < 2 else TT - 1)])
            elif kind == "out" and l == 0:
                s = [1, 2, 0].index(c)
                eng.wait_ge(out_slot if s < 2 else out_mm, s + 1 if s < 2 else 6)
            elif kind == "out":
                eng.wait_ge(out_mm, 6 + OUT_NO[("out", c, 5)])
            else:
                eng.wait_ge(expert_free[c % 6 // 2], PAIRS * l + c // 6 + 1)

        block = ctx.enter_context(nc.Block())

        @block.sync
        def _(sp):
            def fill(i, src):
                sp.dma_start(wslot(i), src).then_inc(ring_loaded[PLACE[i]], 16)

            def free(i):
                if BEFORE[i] is not None:
                    released(sp, BEFORE[i])

            def expert(l, p, j):
                e = 2 * p + j % 2
                w = (w_gate, w_up, w_down)[j // 2][l].rearrange("e (k q) n -> e q k n", q=P)
                return w[e]

            for i, (kind, l, c) in enumerate(STREAM):
                if kind != "moe":
                    free(i)
                    if kind == "mod":
                        src = mod_w[l][:, c * 512:(c + 1) * 512].rearrange("(k q) n -> q k n", q=P)
                    elif kind == "in":
                        o = c * 512 if l == 0 else STEP_COL[c[0]] + 512 * int(c[1])
                        src = in_w[l][:, o:o + 512].rearrange("(k q) n -> q k n", q=P)
                    else:
                        src = out_w[l][c * 512:(c + 1) * 512, :].rearrange("(k q) n -> q k n", q=P)
                    fill(i, src)
                elif c == 0:
                    for j in range(6):
                        free(i + j)
                        if j == 5 or (l == 1 and j == 4):
                            sp.wait_ge(x_ready, TT * (2 * l + 1))
                        fill(i + j, expert(l, 0, j))
                    with sp.Fori(1, PAIRS) as p:
                        for j in range(6):
                            sp.wait_ge(expert_free[j // 2], p + PAIRS * l)
                            fill(i + j, expert(l, p, j))
            for t in range(TT):
                sp.wait_ge(y_ready, t + 1)
                sp.dma_start(y_out[t * P:(t + 1) * P, :], h[:, t, :]).then_inc(y_stored, 16)
            sp.wait_ge(y_stored, 16 * TT)

        @block.tensor
        def _(pe):
            def modulation(l, chunks):
                def columns(g):
                    pe.wait_ge(mod_copied, g + 1)
                    for i in range(4):
                        o = ((g % 12) * 4 + i) * 2
                        mm = pe.matmul(PS[:, MOD_COLS[l], o:o + 2], modrow[:, g % 2, i * P:(i + 1) * P],
                                       C[:, C_SEL2:C_SEL2 + 2], start=True, stop=True)
                    mm.then_inc(mod_col_mm, 1)

                for c in chunks:
                    g = 12 * l + c
                    i = INDEX[("mod", l, c)]
                    arrived(pe, i)
                    need(pe, mod_copied, g - 1)
                    for kk in range(2):
                        for j in range(4):
                            k = 4 * kk + j
                            mm = pe.matmul(PS[32 * j:32 * j + 32, MOD_BANK[l] + g % 2, :], cond[:, k, :],
                                           wslot(i)[:, k, :], start=kk == 0, stop=kk == 1)
                    mm.then_inc(mod_mm, 1)
                    if c:
                        columns(g - 1)
                if chunks[-1] == 11:
                    columns(12 * l + 11)

            def norm_turn(s):
                need(pe, x_ready, TT * s)
                for t in range(TT):
                    pe.wait_ge(xn_ready, TT * s + t + 1)
                    for half in range(2):
                        if t == 2:
                            pe.wait_ge(hT_act if half else hT_dve, TT * s + 1)
                        for i in range(4):
                            k = 4 * half + i
                            mm = pe.transpose(PS[:, 4 + 2 * (t % 2) + half, i * P:(i + 1) * P],
                                              xn[:, t, k * P:(k + 1) * P], ident)
                        mm.then_inc(xnT_mm, 1)
                pe.wait_ge(hT_dve, TT * (s + 1))
                pe.wait_ge(hT_act, TT * (s + 1))

            def gate_rows(s, banks):
                for c in range(2):
                    pe.wait_ge(diag_ready, 2 * s + c + 1)
                    for half in range(2):
                        if len(banks) == 2 and c:
                            pe.wait_ge(gate_copied, 4 * s + half + 1)
                        pe.matmul(PS[:, banks[(2 * c + half) % len(banks)], :], ones,
                                  diags[s][:, c, 4 * half:4 * half + 4, :].rearrange("p a b -> p (a b)"),
                                  start=True, stop=True).then_inc(gate_mm, 1)

            def project(key, lhs, rhs, out, last=KD):
                for k in range(last):
                    mm = pe.matmul(out, lhs(k), rhs(k), start=k == 0, stop=k == last - 1)
                return mm

            pe.wait_ge(cond_ready, 2)
            modulation(0, range(12))
            pe.wait_ge(gain_ready, 1)
            norm_turn(0)
            for c in range(2):
                i = INDEX[("in", 0, c)]
                arrived(pe, i)
                for b in range(CB):
                    project(0, lambda k: wslot(i)[:, k, b * P:(b + 1) * P], lambda k: hT[:, k, :],
                            PS[:, 4 * c + b, 0:NT]).then_inc(proj_mm, 1)
            for n in range(3 * TT):
                i = INDEX[("in", 0, 2 + n // TT)]
                arrived(pe, i)
                if n < 3:
                    pe.wait_ge(glu_done, n + 1)
                else:
                    pe.wait_ge(qk_copied, n - 2)
                project(0, lambda k: hT[:, k, cols(n % TT)], lambda k: wslot(i)[:, k, :],
                        PS[:, n % 3, :]).then_inc(proj_mm, 1)
            pe.wait_ge(glu_done, CB)
            pe.wait_ge(sig_done, CB)
            gate_rows(0, [3, 4, 5, 6])
            pe.wait_ge(gate_copied, 4)
            pe.wait_ge(cache_loaded, 64)
            for t in range(TT):
                pe.wait_ge(qk_ready, t + 1)
                for b in range(3):
                    if t == 0:
                        pe.wait_ge(qk_copied, 3 * TT)
                    else:
                        pe.wait_ge(qkT_act if b < 2 else qkT_dve, 2 * (t - 1) + b + 1 if b < 2 else t)
                    for i in range(4 if b < 2 else KH):
                        mm = pe.transpose(PS[:, b, i * P:(i + 1) * P], qk[:, t, 4 * b + i, :], ident)
                    if t == 0 and b == 2:
                        for i in range(KH):
                            mm = pe.transpose(PS[:, b, (KH + i) * P:(KH + i + 1) * P], kc[:, i, :], ident)
                    mm.then_inc(qkT_mm, 1)
            pe.wait_ge(qkT_act, 2 * TT)
            pe.wait_ge(qkT_dve, TT)
            for u in range(TT * QH + 2):
                if u < TT * QH:
                    t, hd = u // QH, u % QH
                    need(pe, exp_done, u - 1)
                    keys = kT[:, hd // QPK, 0:1, :] if t == 0 else kT[:, hd // QPK, 1:4, :]
                    n = P if t == 0 else 3 * P
                    pe.matmul(PS[:, 3 + u % 2, 0:n], qT[:, hd, cols(t)], keys.rearrange("p a b -> p (a b)"),
                              start=True, stop=True).then_inc(s_mm, 1)
                    if u % 2 == 0:
                        modulation(1, [u // 2])
                if 1 <= u <= TT * QH:
                    w = u - 1
                    pe.wait_ge(pr_ready, w + 1)
                    need(pe, prT_copied, w - 1)
                    for i in range(1 if w < QH else 3):
                        mm = pe.transpose(PS[:, 5 + w % 2, i * P:(i + 1) * P], pr[:, w % 2, i * P:(i + 1) * P], ident)
                    mm.then_inc(prT_mm, 1)
                if u >= 2:
                    w = u - 2
                    t, hd = w // QH, w % QH
                    pe.wait_ge(prT_copied, w + 1)
                    if w % 4 == 0:
                        need(pe, o_copied, w // 4)
                    tiles = [0] if t == 0 else [1, 2, 3]
                    for i, kt in enumerate(tiles):
                        mm = pe.matmul(PS[:, 7, (w % 4) * P:(w % 4 + 1) * P],
                                       vv[:, kt, hd // QPK, :], prT[:, w % 2, i * P:(i + 1) * P],
                                       start=i == 0, stop=i == len(tiles) - 1)
                    if w % 4 == 3:
                        mm.then_inc(o_mm, 1)
            pe.wait_ge(conv_dve, 1)
            pe.wait_ge(conv_pool, 1)
            pe.wait_ge(o_copied, 2 * TT)
            pe.wait_ge(mod_ready, 2)

            def conv_tokens(t):
                if t == 2:
                    pe.wait_ge(z_ready, 1)
                for b in range(CB):
                    mm = pe.transpose(PS[:, 6 + t % 2, b * P:(b + 1) * P], cv[:, b, TOKCOL[t]:TOKCOL[t] + P], ident)
                mm.then_inc(ln_mm, 1)

            def conv_back(t):
                pe.wait_ge(z_ready, (2, 3, 3)[t])
                if t == 2:
                    pe.wait_ge(aT_ready, 1)
                for b in range(CB):
                    mm = pe.transpose(PS[:, (7, 6, 7)[t], b * P:(b + 1) * P], z[:, t, b * P:(b + 1) * P], ident)
                mm.then_inc(zT_mm, 1)

            def out0(n):
                i = INDEX[("out", 0, (1, 2, 0)[n])]
                arrived(pe, i)
                for t in range(TT):
                    if n == 2:
                        pe.wait_ge(aT_ready, t + 1)
                    for half in range(2):
                        for k in range(4):
                            lhs = aT[:, k, cols(t)] if n == 2 else oT[:, 4 * n + k, cols(t)]
                            mm = pe.matmul(PS[:, 2 * t + half, :], lhs, wslot(i)[:, k, half * 512:half * 512 + 512],
                                           start=n == 0 and k == 0, stop=n == 2 and k == 3)
                        if n == 2:
                            mm.then_inc(out_mm, 1)
                if n < 2:
                    mm.then_inc(out_slot, 1)

            conv_tokens(0)
            conv_tokens(1)
            out0(0)
            conv_tokens(2)
            conv_back(0)
            out0(1)
            conv_back(1)
            conv_back(2)
            out0(2)

            def experts(l):
                s = 2 * l + 1
                norm_turn(s)
                for t in range(TT):
                    for k in range(KD):
                        o = V_RW + 160 * l + 20 * k
                        mm = pe.matmul(PS[:, 2, 20 * t:20 * t + 20], hT[:, k, cols(t)], V[:, o:o + 20],
                                       start=k == 0, stop=k == KD - 1)
                mm.then_inc(router_mm, 1)
                for t in range(TT):
                    for half in range(2):
                        if t == 2:
                            pe.wait_ge(h_copied, 6 * l + half + 1)
                        for i in range(4):
                            mm = pe.transpose(PS[:, 4 + 2 * (t % 2) + half, i * P:(i + 1) * P],
                                              hT[:, 4 * half + i, cols(t)], ident)
                        mm.then_inc(hback_mm, 1)
                gate_rows(s, [0, 1])
                pe.wait_ge(mem_ready, l + 1)
                for t in range(TT):
                    for v in range(t + 1):
                        mm = pe.matmul(PS[:, 3, 16 * t:16 * t + 16], C[:, C_UPPER:C_UPPER + P] if v == t else ones,
                                       mem[:, v, :], start=v == 0, stop=v == t)
                for v in range(TT):
                    mm = pe.matmul(PS[:, 3, 48:64], ones, mem[:, v, :], start=v == 0, stop=v == TT - 1)
                mm.then_inc(rank_mm, 1)
                pe.wait_ge(counts_ready, l + 1)
                pe.wait_ge(h_copied, 6 * l + 6)
                pe.wait_ge(gate_copied, 4 * s + 4)
                first = INDEX[("moe", l, 0)]
                W = [wslot(first + j) for j in range(6)]
                B8, B5 = PAIRS * l, 5 * PAIRS * l
                S0 = (6 * PAIRS + 1) * l + 1

                def here(p, j):
                    pe.wait_ge(ring_loaded[j], 16 * p + 16 * (USES[first + j] + 1))

                def gather(dst):
                    for half in range(2):
                        for i in range(4):
                            k = 4 * half + i
                            for t in range(TT):
                                mm = pe.matmul(PS[:, 2 + half, i * P:(i + 1) * P], h[:, t, k * P:(k + 1) * P],
                                               sel[:, t, :], start=t == 0, stop=t == TT - 1)
                        if dst:
                            mm.then_inc(gath_mm, 1)
                    return mm

                def up(j, g):
                    for k in range(KD):
                        for e in range(2):
                            mm = pe.matmul(PS[64 * e:64 * e + 64, j, :], g[:, k, 64 * e:64 * e + 64],
                                           W[2 * j + e][:, k, :], start=k == 0, stop=k == KD - 1)
                    return mm

                def hid_turn():
                    for i in range(4):
                        mm = pe.transpose(PS[:, 4, i * P:(i + 1) * P], hid[:, i * P:(i + 1) * P], ident)
                    return mm

                def down(half):
                    for k in range(4):
                        for e in range(2):
                            mm = pe.matmul(PS[64 * e:64 * e + 64, 5 + half, :], hidT[:, k, 64 * e:64 * e + 64],
                                           W[4 + e][:, k, half * 512:half * 512 + 512], start=k == 0, stop=k == 3)
                    return mm

                def scatter(p):
                    pe.wait_ge(y_copied, 2 * p + 2 * (B8 + 1))
                    pe.wait_ge(selT_copied, p + B8 + 1)
                    for i in range(6):
                        if i >= 2:
                            pe.wait_ge(acc_add, 6 * p + S0 + i - 1)
                        pe.matmul(PS[:, i % 2, :], selT[:, i // 2, :], ysb[:, (i % 2) * 512:(i % 2) * 512 + 512],
                                  start=True, stop=True).then_inc(scat_mm, 1)

                def overflow(step):
                    pe.wait_ge(ov_dve, 3 * step + 1)
                    for t in range(TT):
                        pe.transpose(PS[:, 7, t * P:(t + 1) * P], selw[:, t, :], ident)
                    gather(None).then_inc(ov_pe, 1)
                    pe.wait_ge(ov_act, 4 * step + 1)
                    up(0, gT_ov)
                    up(1, gT_ov).then_inc(ov_pe, 1)
                    pe.wait_ge(ov_dve, 3 * step + 2)
                    hid_turn().then_inc(ov_pe, 1)
                    pe.wait_ge(ov_act, 4 * step + 3)
                    down(0)
                    down(1).then_inc(ov_pe, 1)
                    pe.wait_ge(ov_act, 4 * step + 4)
                    for i, b in enumerate((0, 1, 2, 3, 5, 6)):
                        mm = pe.matmul(PS[:, b, :], selT_ov[:, i // 2, :],
                                       y_ov[:, (i % 2) * 512:(i % 2) * 512 + 512], start=True, stop=True)
                    mm.then_inc(ov_pe, 1)
                    pe.wait_ge(ov_dve, 3 * step + 3)

                def pair(p, first_pair=False, last_pair=False):
                    pe.wait_ge(gath_copied, 2 * p + 2 * (B8 + 1))
                    if not first_pair:
                        pe.wait_ge(acc_add, 6 * p + S0 - 6)
                    here(p, 0)
                    here(p, 1)
                    up(0, gT).then_inc(egate_mm, 1)
                    here(p, 2)
                    here(p, 3)
                    up(1, gT).then_inc(eup_mm, 1)
                    if not last_pair:
                        pe.wait_ge(sel_ready, p + B8 + 2)
                        gather(1)
                    n = pe.value_load(counts[0:1, bass.ds(p, 1)], min_val=0, max_val=NT)
                    pe.wait_ge(hid_ready, p + B8 + 1)
                    hid_turn().then_inc(hidT_mm, 1)
                    if not first_pair:
                        scatter(p - 1)
                    pe.wait_ge(selw_ready, p + B8 + 1)
                    for t in range(TT):
                        mm = pe.transpose(PS[:, 7, t * P:(t + 1) * P], selw[:, t, :], ident)
                    mm.then_inc(selT_mm, 1)
                    pe.wait_ge(hidT_copied, p + B8 + 1)
                    here(p, 4)
                    here(p, 5)
                    for half in range(2):
                        down(half).then_inc(down_mm, 1)
                    with pe.If(n > CAP):
                        if not first_pair:
                            pe.wait_ge(acc_add, 6 * p + S0)
                        pe.wait_ge(gath_copied, 2 * p + 2 * (B8 + (1 if last_pair else 2)))
                        pe.wait_ge(y_copied, 2 * p + 2 * (B8 + 1))
                        pe.wait_ge(selT_copied, p + B8 + 1)
                        overflow(5 * p + B5)
                        with pe.If(n > 2 * CAP):
                            with pe.Fori(1, UNITS - 1) as u:
                                overflow(5 * p + B5 + u)
                        with pe.Else():
                            pe.wait_ge(ov_pe, 25 * p + 5 * (B5 + 1))
                            pe.sem_inc(ov_pe, 5 * (UNITS - 2))
                        pe.nop()
                    with pe.Else():
                        need(pe, ov_pe, 25 * p + 5 * B5)
                        pe.sem_inc(ov_pe, 5 * (UNITS - 1))
                    pe.nop()

                pe.wait_ge(sel_ready, B8 + 1)
                gather(1)
                pair(0, first_pair=True)
                with pe.Fori(1, PAIRS - 1) as p:
                    pair(p)
                pair(PAIRS - 1, last_pair=True)
                pe.wait_ge(acc_add, 6 * (PAIRS - 1) + S0)
                scatter(PAIRS - 1)

            experts(0)

            norm_turn(2)
            for ev in RET:
                kind, a, b = ev
                if kind in ("job", "out"):
                    n = UNTIL[ev]
                    if n >= 3:
                        before = SHARED[n - 3]
                        if before[0] == "job":
                            pe.wait_ge(job_copied, COPY_NO[before])
                        else:
                            pe.wait_ge(out_add, OUT_NO[before])
                if kind == "job":
                    i = INDEX[("in", 1, a)]
                    arrived(pe, i)
                    project(1, lambda k: hT[:, k, cols(b)], lambda k: wslot(i)[:, k, :],
                            PS[:, n % 3, :]).then_inc(proj_mm, 1)
                elif kind == "out":
                    i = INDEX[("out", 1, a)]
                    arrived(pe, i)
                    t, half = b // 2, b % 2
                    pe.wait_ge(mixT_copied, 2 * (2 * a + 2))
                    project(1, lambda k: mixT[:, k, cols(t)], lambda k: wslot(i)[:, k, half * 512:half * 512 + 512],
                            PS[:, n % 3, :], 4).then_inc(out_mm, 1)
                elif kind == "gate":
                    gate_rows(2, [3, 4, 5, 6])
                elif kind == "turn":
                    if a == 0:
                        pe.wait_ge(gate_copied, 12)
                    pe.wait_ge(job_copied, COPY_NO[("job", f"k{a}", 2)])
                    pe.wait_ge(rope_done, ROPE_NO[("job", f"k{a}", 2)])
                    for t in range(TT):
                        for j, src in enumerate((qtok, ktok)):
                            need(pe, turn_copied, 6 * a + 2 * t + j - 1 if t else 0)
                            for i in range(4):
                                mm = pe.transpose(PS[:, 3 + j, i * P:(i + 1) * P], src[:, t, i * P:(i + 1) * P], ident)
                            mm.then_inc(turn_mm, 1)
                elif kind == "A":
                    v = v1[a // 2 % 2]
                    o = (a % 2) * DV
                    pe.wait_ge(turn_copied, 6 * (a // 4 + 1))
                    need(pe, yr_ready, TT * a)
                    for t in range(TT):
                        mm = pe.matmul(PS[:, 3, cols(t)], k1T[:, a % 4, cols(t)], q1T[:, a % 4, cols(t)],
                                       start=True, stop=True)
                    mm.then_inc(rA_mm, 1)
                    pe.wait_ge(kd_ready, a + 1)
                    pe.wait_ge(job_copied, COPY_NO[("job", f"v{a // 2}", 2)])
                    for i, t in enumerate((0, 0, 1, 2)):
                        mm = pe.matmul(PS[:, 4 + i // 2, (i % 2) * DV:(i % 2 + 1) * DV], kd[:, i, :], v[:, t, o:o + DV],
                                       start=True, stop=True)
                        if i % 2:
                            mm.then_inc(rA_mm, 1)
                elif kind == "B":
                    v = v1[a // 2 % 2]
                    o = (a % 2) * DV
                    pe.wait_ge(smask_ready, a + 1)
                    need(pe, mixT_copied, 2 * a)
                    pe.wait_ge(st1_ready, a + 1)
                    pe.wait_ge(stout_ready, a + 1)
                    for t in range(TT):
                        own, state = ((6, None), (7, 3), (4, 5))[t]
                        for d in range(2):
                            mm = pe.matmul(PS[:, own, d * DV:(d + 1) * DV], smask[:, d, t, :], v[:, t, o:o + DV],
                                           start=True, stop=True)
                        if t:
                            for d in range(2):
                                s0 = st0[:, a % 2, d, :] if t == 1 + d else st1[:, d, :]
                                mm = pe.matmul(PS[:, state, d * DV:(d + 1) * DV], q1T[:, a % 4, cols(t)], s0,
                                               start=True, stop=True)
                        mm.then_inc(rB_mm, 1)
                elif kind == "C":
                    pe.wait_ge(mix_ready, a + 1)
                    for t in range(TT):
                        for i in range(2):
                            mm = pe.transpose(PS[:, 6 + t // 2, (t % 2 * 2 + i) * P:(t % 2 * 2 + i + 1) * P],
                                              mix[:, t, i * P:(i + 1) * P], ident)
                        if t:
                            mm.then_inc(mixT_mm, 1)
            experts(1)

        @block.scalar
        def _(act):
            def mod_copies(l, chunks):
                for c in chunks:
                    g = 12 * l + c
                    act.wait_ge(mod_mm, g + 1)
                    need(act, mod_col_mm, g - 1)
                    act.activation(modrow[:, g % 2, :], PS[:, MOD_BANK[l] + g % 2, :], ACT.Copy).then_inc(mod_copied, 1)

            def norm_stats(s, t):
                if s == 0:
                    act.wait_ge(x_loaded[t], 16)
                else:
                    act.wait_ge(x_ready, TT * (s - 1) + t + 1)
                act.activation(junk, x[:, t, :], ACT.Square, accum_out=stat[:, t:t + 1]).then_inc(sumsq, 1)
                act.wait_ge(sumsq, TT * s + t + 1)
                act.activation(stat[:, 4 + t:5 + t], stat[:, t:t + 1], ACT.Sqrt, bias=eps, scale=1.0 / D).then_inc(rms, 1)

            def norm_evac(s, t):
                l, shift = s // 2, 24 * (s % 2)
                act.wait_ge(xnT_mm, 2 * (TT * s + t) + 2)
                act.wait_ge(gain_ready, l + 1)
                for i in range(4):
                    k = 4 + i
                    a = act.activation(hT[:, k, cols(t)], PS[:, 5 + 2 * (t % 2), i * P:(i + 1) * P], ACT.Identity,
                                       bias=modc[:, l, shift + k, cnd(t):cnd(t) + 1], scale=gain[:, s, k, cnd(t):cnd(t) + 1])
                a.then_inc(hT_act, 1)

            def norm(s):
                norm_stats(s, 0)
                norm_stats(s, 1)
                norm_evac(s, 0)
                norm_stats(s, 2)
                norm_evac(s, 1)
                norm_evac(s, 2)

            def gate_copies(s, banks):
                for i in range(4):
                    act.wait_ge(gate_mm, 4 * s + i + 1)
                    act.activation(gate_row[:, i // 2, (i % 2) * 512:(i % 2) * 512 + 512],
                                   PS[:, banks[i % len(banks)], :], ACT.Copy).then_inc(gate_copied, 1)

            act.dma_start(V[:, :], par).then_inc(par_loaded, 16)
            act.dma_start(C[:, :], cst).then_inc(par_loaded, 16)
            act.wait_ge(par_loaded, 32)
            act.wait_ge(cond_ready, 1)
            act.activation(cond[:, :, 0:2], V[:, V_COND:V_COND + 16].rearrange("p (k c) -> p k c", c=2),
                           ACT.Silu).then_inc(cond_ready, 1)
            mod_copies(0, range(4))
            for t in range(TT):
                act.dma_start(x[:, t, :], x_in[t * P:(t + 1) * P, :]).then_inc(x_loaded[t], 16)
            for i in range(KH):
                act.dma_start(kc[:, i, :], cache_k[i]).then_inc(cache_loaded, 16)
                act.dma_start(vv[:, 1, i, :], cache_v[i]).then_inc(cache_loaded, 16)
            mod_copies(0, range(4, 12))
            norm(0)
            for b in range(CB):
                act.wait_ge(proj_mm, JOBS[(0, 1, b)])
                act.activation(sig[:, b, :], PS[:, 4 + b, 0:NT], ACT.Sigmoid).then_inc(sig_done, 1)
            for n in range(3 * TT):
                c, t = n // TT, n % TT
                act.wait_ge(proj_mm, JOBS[(0, 2 + c, t)])
                if c < 2:
                    act.activation(qk[:, t, 4 * c:4 * c + 4, :].rearrange("p a b -> p (a b)"), PS[:, n % 3, :],
                                   ACT.Copy).then_inc(qk_copied, 1)
                else:
                    act.activation(qk[:, t, QH:HQK, :].rearrange("p a b -> p (a b)"), PS[:, n % 3, 0:KH * HD], ACT.Copy)
                    act.activation(vv[:, (0, 2, 3)[t], :, :].rearrange("p a b -> p (a b)"), PS[:, n % 3, KH * HD:512],
                                   ACT.Copy).then_inc(qk_copied, 1)
            for i in range(KH):
                act.wait_ge(qk_copied, 2 * TT + 1)
                act.dma_start(new_v[i], vv[:, 0, i, :]).then_inc(kv_out, 16)
            gate_copies(0, [3, 4, 5, 6])
            for t in range(TT):
                act.wait_ge(qk_sq, t + 1)
                act.activation(stat[:, 16 + HQK * (t % 2):16 + HQK * (t % 2) + HQK], stat[:, 36:36 + HQK], ACT.Sqrt,
                               bias=eps, scale=1.0 / HD).then_inc(qk_rms, 1)
            for t in range(TT):
                for b in range(2):
                    act.wait_ge(qkT_mm, 3 * t + b + 1)
                    act.activation(qT[:, 4 * b:4 * b + 4, cols(t)], PS[:, b, :].rearrange("p (a b) -> p a b", a=4),
                                   ACT.Copy).then_inc(qkT_act, 1)
            for i in range(KH):
                act.wait_ge(qk_ready, 1)
                act.dma_start(new_k[i], qk[:, 0, QH + i, :]).then_inc(kv_out, 16)
            for u in range(TT * QH + 2):
                if u < TT * QH:
                    n = P if u < QH else 3 * P
                    act.wait_ge(s_max, u + 1)
                    need(act, prT_mm, u - 1)
                    act.activation(pr[:, u % 2, 0:n], PS[:, 3 + u % 2, 0:n], ACT.Exp, bias=stat[:, 46 + u % 2:47 + u % 2],
                                   scale=HD ** -0.5, accum_out=stat[:, 48 + u % 2:49 + u % 2]).then_inc(exp_done, 1)
                    if u % 2 == 0:
                        mod_copies(1, [u // 2])
                if 1 <= u <= TT * QH:
                    w = u - 1
                    n = P if w < QH else 3 * P
                    act.wait_ge(prT_mm, w + 1)
                    act.activation(prT[:, w % 2, 0:n], PS[:, 5 + w % 2, 0:n], ACT.Copy).then_inc(prT_copied, 1)
                if u >= 2 and (u - 2) % 4 == 3:
                    g = (u - 2) // 4
                    act.wait_ge(o_mm, g + 1)
                    act.activation(oT[:, 4 * (g % 2):4 * (g % 2) + 4, cols(g // 2)],
                                   PS[:, 7, :].rearrange("p (a b) -> p a b", a=4),
                                   ACT.Copy).then_inc(o_copied, 1)
            for t in range(TT):
                act.wait_ge(ln_var, t + 1)
                act.activation(stat[:, 58 + t % 2:59 + t % 2], stat[:, 57:58], ACT.Sqrt, bias=eps).then_inc(ln_std, 1)
            for t in range(TT):
                act.wait_ge(zT_mm, t + 1)
                for b in range(CB):
                    a = act.activation(aT[:, b, cols(t)], PS[:, (7, 6, 7)[t], b * P:(b + 1) * P], ACT.Silu,
                                       bias=V[:, V_CNB + b:V_CNB + b + 1], scale=V[:, V_CNG + b:V_CNG + b + 1])
                a.then_inc(aT_ready, 1)

            def experts(l):
                s = 2 * l + 1
                norm(s)
                for i in range(6):
                    if i == 2:
                        act.wait_ge(route_d, 2 * l + 1)
                        act.activation(ge, gd, ACT.Exp).then_inc(route_e, 1)
                    act.wait_ge(hback_mm, 6 * l + i + 1)
                    act.activation(h[:, i // 2, (i % 2) * 512:(i % 2) * 512 + 512], PS[:, 4 + i % 4, :],
                                   ACT.Copy).then_inc(h_copied, 1)
                act.wait_ge(route_d, 2 * l + 2)
                act.activation(rs[:, 6, :], rs[:, 5, :], ACT.Exp).then_inc(route_e, 1)
                gate_copies(s, [0, 1])
                act.wait_ge(counts_ready, l + 1)
                B8, B5 = PAIRS * l, 5 * PAIRS * l
                S0 = (6 * PAIRS + 1) * l + 1

                def copy2(dst, bank):
                    for half in range(2):
                        a = act.activation(dst[:, half * 512:half * 512 + 512], PS[:, bank + half, :], ACT.Copy)
                    return a

                def gathered(p):
                    for half in range(2):
                        act.wait_ge(gath_mm, 2 * p + 2 * B8 + half + 1)
                        act.activation(gT[:, 4 * half:4 * half + 4, :].rearrange("p a b -> p (a b)"), PS[:, 2 + half, :],
                                       ACT.Copy).then_inc(gath_copied, 1)

                def overflow(step):
                    act.wait_ge(ov_pe, 5 * step + 1)
                    act.activation(selT_ov.rearrange("p a b -> p (a b)"), PS[:, 7, 0:NT], ACT.Copy)
                    copy2(gT_ov.rearrange("p a b -> p (a b)"), 2).then_inc(ov_act, 1)
                    act.wait_ge(ov_pe, 5 * step + 2)
                    act.activation(sgate, PS[:, 0, :], ACT.Silu).then_inc(ov_act, 1)
                    act.wait_ge(ov_pe, 5 * step + 3)
                    act.activation(hidT.rearrange("p a b -> p (a b)"), PS[:, 4, :], ACT.Copy).then_inc(ov_act, 1)
                    act.wait_ge(ov_pe, 5 * step + 4)
                    copy2(y_ov, 5).then_inc(ov_act, 1)

                def pair(p, last_pair=False):
                    n = act.value_load(counts[0:1, bass.ds(p, 1)], min_val=0, max_val=NT)
                    act.wait_ge(egate_mm, p + B8 + 1)
                    act.activation(sgate, PS[:, 0, :], ACT.Silu).then_inc(silu_done, 1)
                    with act.If(n < CAP + 1):
                        act.sem_inc(expert_free[0], 1)
                        act.wait_ge(eup_mm, p + B8 + 1)
                        act.sem_inc(expert_free[1], 1)
                    if not last_pair:
                        gathered(p + 1)
                    act.wait_ge(hidT_mm, p + B8 + 1)
                    act.activation(hidT.rearrange("p a b -> p (a b)"), PS[:, 4, :], ACT.Copy).then_inc(hidT_copied, 1)
                    act.wait_ge(selT_mm, p + B8 + 1)
                    act.activation(selT.rearrange("p a b -> p (a b)"), PS[:, 7, 0:NT], ACT.Copy).then_inc(selT_copied, 1)
                    for half in range(2):
                        act.wait_ge(down_mm, 2 * p + 2 * B8 + half + 1)
                        act.activation(ysb[:, half * 512:half * 512 + 512], PS[:, 5 + half, :],
                                       ACT.Copy).then_inc(y_copied, 1)
                    with act.If(n > CAP):
                        overflow(5 * p + B5)
                        with act.If(n > 2 * CAP):
                            with act.Fori(1, UNITS - 1) as u:
                                overflow(5 * p + B5 + u)
                        with act.Else():
                            act.wait_ge(ov_act, 20 * p + 4 * (B5 + 1))
                            act.sem_inc(ov_act, 4 * (UNITS - 2))
                        for s in expert_free:
                            act.sem_inc(s, 1)
                    with act.Else():
                        act.sem_inc(expert_free[2], 1)
                        need(act, ov_act, 20 * p + 4 * B5)
                        act.sem_inc(ov_act, 4 * (UNITS - 1))
                    act.nop()

                gathered(0)
                pair(0)
                with act.Fori(1, PAIRS - 1) as p:
                    pair(p)
                pair(PAIRS - 1, last_pair=True)

            experts(0)

            norm(2)

            def load_state(a):
                for d in range(2):
                    act.dma_start(st0[:, a % 2, d, :], st_in[d][a]).then_inc(st_loaded[a % 2], 16)

            load_state(0)
            load_state(1)
            act.activation(dec[:, 4, :], V[:, V_DEC:V_DEC + 16], ACT.Exp).then_inc(dec_ready, 1)
            act.wait_ge(dec_ready, 2)
            lgam = dec[:, 4, :]
            for d in range(2):
                for h0, pc in ((0, (0, 1)[d]), (1, (2, 3)[d])):
                    act.activation(dec[:, h0, d * RH:(d + 1) * RH], lgam[:, d * RH:(d + 1) * RH], ACT.Exp,
                                   scale=C[:, C_POS + pc:C_POS + pc + 1])
            act.activation(dec[:, 2, :], lgam, ACT.Exp, scale=float(P)).then_inc(dec_ready, 1)
            for a in range(RH):
                for d in range(2):
                    o = (C_DF, C_DB)[d]
                    i = act.activation(masks[:, a, d, :], C[:, o:o + P], ACT.Exp, scale=lgam[:, d * RH + a:d * RH + a + 1])
                i.then_inc(mask_exp, 1)
            for ev in RET:
                kind, a, b = ev
                if kind == "job":
                    act.wait_ge(proj_mm, JOBS[(1, a, b)])
                    bank, part = UNTIL[ev] % 3, int(a[1])
                    if a == "f1" and b == 0:
                        act.wait_ge(gate_mm, 12)
                    if a[0] == "q":
                        need(act, mix_ready, 4 * part)
                        if part == 0:
                            act.wait_ge(gate_copied, 8)
                    dst = {"q": qtok, "k": ktok, "v": v1[part % 2]}.get(a[0])
                    if a[0] in "fb":
                        dst = sg1[part % 2][:, "fb".index(a[0]), :, :]
                        need(act, mix_ready, 2 * (part - 1))
                    if a[0] == "v":
                        need(act, rB_mm, TT * 2 * (part - 1))
                    if a[0] == "k":
                        need(act, kd_ready, 4 * part)
                    act.activation(dst[:, b, :], PS[:, bank, :], ACT.Silu if a[0] in "fb" else ACT.Copy,
                                   scale=DK ** -0.5 if a[0] == "k" else 1.0).then_inc(job_copied, 1)
                elif kind == "gate":
                    gate_copies(2, [3, 4, 5, 6])
                elif kind == "turn":
                    for t in range(TT):
                        for j, dst in enumerate((q1T, k1T)):
                            act.wait_ge(turn_mm, 6 * a + 2 * t + j + 1)
                            act.activation(dst[:, :, cols(t)], PS[:, 3 + j, :].rearrange("p (a b) -> p a b", a=4),
                                           ACT.Copy).then_inc(turn_copied, 1)
                elif kind == "A":
                    act.wait_ge(rA_mm, 3 * a + 2)
                    need(act, state_out, 32 * a)
                    act.activation(stout.rearrange("p a b -> p (a b)"), PS[:, 4, :], ACT.Copy).then_inc(stout_ready, 1)
                    act.wait_ge(stout_ready, a + 1)
                    for d in range(2):
                        act.dma_start(st_out[d][a], stout[:, d, :]).then_inc(state_out, 16)
                elif kind == "B":
                    act.wait_ge(yr_ready, TT * a + TT)
                    for t in range(TT):
                        for d in range(2):
                            out = (mix, smask_v)[d][:, t, :]
                            i = act.activation(out, yr[:, t, d, :], ACT.Square,
                                               accum_out=stat[:, 16 + 2 * t + d:17 + 2 * t + d])
                    i.then_inc(yr_sq, 1)
                    act.wait_ge(yr_sq, a + 1)
                    act.activation(stat[:, 24:30], stat[:, 16:22], ACT.Sqrt, bias=eps, scale=1.0 / DV).then_inc(yr_rms, 1)
                elif kind == "C":
                    o = 2 * (a % 2)
                    if a % 2 == 0:
                        need(act, out_mm, 6 + 6 * (a // 2) if a else 0)
                    act.wait_ge(mixT_mm, 2 * a + 1)
                    for t in range(2):
                        i = act.activation(mixT[:, o:o + 2, cols(t)],
                                           PS[:, 6, t * 2 * P:(t + 1) * 2 * P].rearrange("p (a b) -> p a b", a=2), ACT.Copy)
                    i.then_inc(mixT_copied, 1)
                    act.wait_ge(mixT_mm, 2 * a + 2)
                    act.activation(mixT[:, o:o + 2, cols(2)], PS[:, 7, 0:2 * P].rearrange("p (a b) -> p a b", a=2),
                                   ACT.Copy).then_inc(mixT_copied, 1)
                    if a + 2 < RH:
                        act.wait_ge(st1_ready, a + 1)
                        load_state(a + 2)
            act.wait_ge(state_out, 32 * RH)
            act.wait_ge(kv_out, 64)
            act.wait_ge(x_ready, 9)
            act.dma_start(fg, fgain).then_inc(fg_loaded, 16)
            experts(1)
            for t in range(TT):
                norm_stats(4, t)

        @block.gpsimd
        def _(pool):
            pool.memset(cond, 0.0).then_inc(cond_ready, 1)
            pool.memset(apad, 0.0).then_inc(pad_zero, 1)
            pool.wait_ge(par_loaded, 32)
            pool.wait_ge(glu_done, CB)
            w = V_CW + TAPS * 3
            pool.tensor_scalar(cv[:, 3, :], apad[:, 3, 0:CVN], V[:, w:w + 1], V[:, V_CB + 3:V_CB + 4], ALU.mult,
                               ALU.add).then_inc(pool_chain, 1)
            for j in range(1, TAPS):
                need(pool, pool_chain, 2 * (j - 2) + 1 if j > 2 else 0)
                pool.tensor_scalar(ctap[:, j % 2, :], apad[:, 3, j:j + CVN], V[:, w + j:w + j + 1], None,
                                   ALU.mult).then_inc(pool_chain, 1)
                pool.wait_ge(pool_chain, 2 * j)
                pool.tensor_tensor(cv[:, 3, :], cv[:, 3, :], ctap[:, j % 2, :], ALU.add).then_inc(
                    conv_pool if j == TAPS - 1 else pool_chain, 1)
            pool.wait_ge(x_ready, 3)
            pool.wait_ge(kv_out, 64)
            pool.memset(acc, 0.0).then_inc(acc_add, 1)
            for a in range(RH):
                pool.wait_ge(mask_exp, a + 1)
                i = pool.tensor_tensor(masks[:, a, :, :], masks[:, a, :, :],
                                       C[:, C_MF:C_MF + 2 * P].rearrange("p (a b) -> p a b", a=2), ALU.mult)
                i.then_inc(mask_ready, 1)
            pool.wait_ge(dec_ready, 3)
            for a in range(RH):
                step = f"k{a // 4}"
                pool.wait_ge(job_copied, COPY_NO[("job", step, 2)])
                pool.wait_ge(rope_done, ROPE_NO[("job", step, 2)])
                need(pool, rA_mm, 3 * a)
                for i, (t, d) in enumerate(((0, 0), (0, 1), (1, 0), (2, 1))):
                    o = (a % 4) * P
                    w = pool.tensor_scalar(kd[:, i, :], ktok[:, t, o:o + P], dec[:, 1, d * RH + a:d * RH + a + 1],
                                           None, ALU.mult)
                w.then_inc(kd_ready, 1)
            pool.wait_ge(x_ready, 9)
            pool.wait_ge(state_out, 32 * RH)
            pool.memset(acc, 0.0).then_inc(acc_add, 1)

        @block.vector
        def _(dve):
            links = [0]

            def mark(ins):
                links[0] += 1
                ins.then_inc(dve_chain, 1)
                return links[0]

            def link(ins):
                dve.wait_ge(dve_chain, mark(ins))

            def mod_columns(l):
                dve.wait_ge(mod_col_mm, 12 * (l + 1))
                i = dve.tensor_tensor(modc[:, l, :, :], PS[:, MOD_COLS[l], 0:96].rearrange("p (a b) -> p a b", b=2),
                                      V[:, V_MODB + 48 * l:V_MODB + 48 * l + 48].unsqueeze(2).to_broadcast([P, 48, 2]), ALU.add)
                i.then_inc(mod_ready, 1)
                dve.wait_ge(mod_ready, l + 1)
                for j in range(2):
                    s = 2 * l + j
                    i = dve.scalar_tensor_tensor(gain[:, s, :, :], modc[:, l, 24 * j + 8:24 * j + 16, :], 1.0,
                                                 V[:, V_NG + 8 * s:V_NG + 8 * s + 8].unsqueeze(2).to_broadcast([P, KD, 2]),
                                                 ALU.add, ALU.mult)
                i.then_inc(gain_ready, 1)
                dve.wait_ge(gain_ready, l + 1)

            def norm(s):
                l, shift = s // 2, 24 * (s % 2)

                def scaled(t):
                    dve.wait_ge(rms, TT * s + t + 1)
                    link(dve.reciprocal(stat[:, 8 + t:9 + t], stat[:, 4 + t:5 + t]))
                    dve.tensor_scalar(xn[:, t, :], x[:, t, :], stat[:, 8 + t:9 + t], None, ALU.mult).then_inc(xn_ready, 1)

                def evac(t):
                    dve.wait_ge(xnT_mm, 2 * (TT * s + t) + 1)
                    for k in range(4):
                        i = dve.tensor_scalar(hT[:, k, cols(t)], PS[:, 4 + 2 * (t % 2), k * P:(k + 1) * P],
                                              gain[:, s, k, cnd(t):cnd(t) + 1], modc[:, l, shift + k, cnd(t):cnd(t) + 1],
                                              ALU.mult, ALU.add)
                    i.then_inc(hT_dve, 1)

                scaled(0)
                scaled(1)
                evac(0)
                scaled(2)
                evac(1)
                evac(2)

            def gate_diag(s):
                l, piece = s // 2, 16 + 24 * (s % 2)
                for c in range(2):
                    dve.tensor_tensor(diags[s][:, c, :, :], ident.unsqueeze(1).to_broadcast([P, KD, P]),
                                      modc[:, l, piece:piece + KD, c].unsqueeze(2).to_broadcast([P, KD, P]),
                                      ALU.mult).then_inc(diag_ready, 1)

            def rope(a, b, src, heads, t):
                cos = C[:, C_COS + P * (t - 1):C_COS + P * t].unsqueeze(1).to_broadcast([P, heads, P])
                sin = C[:, C_SIN + P * (t - 1):C_SIN + P * t].rearrange("p (x y j) -> p x y j", x=2, y=2)
                dve.tensor_tensor(a, src, cos, ALU.mult)
                for x in range(2):
                    s4 = src[:, :, 64 * x:64 * x + 64].rearrange("p h (y j) -> p h y j", y=2)
                    b4 = b[:, :, 64 * x:64 * x + 64].rearrange("p h (y j) -> p h y j", y=2)
                    for y in range(2):
                        i = dve.tensor_tensor(b4[:, :, y, :], s4[:, :, 1 - y, :],
                                              sin[:, x, y, :].unsqueeze(1).to_broadcast([P, heads, 32]), ALU.mult)
                link(i)
                return dve.tensor_tensor(src, a, b, ALU.add)

            dve.wait_ge(par_loaded, 32)
            mod_columns(0)
            norm(0)
            gate_diag(0)
            dve.wait_ge(pad_zero, 1)
            for b in range(CB):
                dve.wait_ge(sig_done, b + 1)
                dve.wait_ge(proj_mm, JOBS[(0, 0, b)])
                dve.tensor_tensor(apad[:, b, CTX0:CTX0 + P], PS[:, b, 0:P], sig[:, b, 0:P], ALU.mult)
                dve.tensor_tensor(apad[:, b, LAT0:LAT0 + 2 * P], PS[:, b, P:NT], sig[:, b, P:NT],
                                  ALU.mult).then_inc(glu_done, 1)
            last = [None] * 3

            def conv_tap(b, j):
                o = V_CW + TAPS * b + j
                if j == 0:
                    i = dve.tensor_scalar(cv[:, b, :], apad[:, b, 0:CVN], V[:, o:o + 1], V[:, V_CB + b:V_CB + b + 1],
                                          ALU.mult, ALU.add)
                else:
                    dve.wait_ge(dve_chain, last[b])
                    i = dve.scalar_tensor_tensor(cv[:, b, :], apad[:, b, j:j + CVN], V[:, o:o + 1], cv[:, b, :],
                                                 ALU.mult, ALU.add)
                if b == 2 and j == TAPS - 1:
                    i.then_inc(conv_dve, 1)
                else:
                    last[b] = mark(i)

            dve.wait_ge(glu_done, 3)
            for j in range(TAPS):
                for b in range(2):
                    conv_tap(b, j)
            for t in range(TT):
                dve.wait_ge(qk_copied, 2 * TT + t + 1)
                r0 = 16 + HQK * (t % 2)
                need(dve, qk_ready, t)
                link(dve.tensor_tensor(tmp2[:, 0], qk[:, t], qk[:, t], ALU.mult))
                dve.tensor_reduce(stat[:, 36:36 + HQK], tmp2[:, 0], AX, ALU.add).then_inc(qk_sq, 1)
                dve.wait_ge(qk_rms, t + 1)
                link(dve.reciprocal(stat[:, r0:r0 + HQK], stat[:, r0:r0 + HQK]))
                link(dve.tensor_tensor(qk[:, t], qk[:, t], stat[:, r0:r0 + HQK].unsqueeze(2).to_broadcast([P, HQK, HD]), ALU.mult))
                dve.tensor_tensor(qk[:, t, 0:QH], qk[:, t, 0:QH], V[:, V_QKG:V_QKG + HD].unsqueeze(1).to_broadcast([P, QH, HD]), ALU.mult)
                i = dve.tensor_tensor(qk[:, t, QH:HQK], qk[:, t, QH:HQK],
                                      V[:, V_QKG + HD:V_QKG + 2 * HD].unsqueeze(1).to_broadcast([P, KH, HD]), ALU.mult)
                if t:
                    link(i)
                    i = rope(tmp2[:, 0], tmp2[:, 1], qk[:, t], HQK, t)
                i.then_inc(qk_ready, 1)
            for t in range(TT):
                dve.wait_ge(qkT_mm, 3 * t + 3)
                i = dve.tensor_copy(kT[:, :, (0, 2, 3)[t], :], PS[:, 2, 0:KH * P].rearrange("p (a b) -> p a b", a=KH))
                if t == 0:
                    i = dve.tensor_copy(kT[:, :, 1, :], PS[:, 2, KH * P:2 * KH * P].rearrange("p (a b) -> p a b", a=KH))
                i.then_inc(qkT_dve, 1)
            for u in range(TT * QH + 1):
                if u < TT * QH:
                    n = P if u < QH else 3 * P
                    dve.wait_ge(s_mm, u + 1)
                    link(dve.tensor_reduce(stat[:, 50 + u % 2:51 + u % 2], PS[:, 3 + u % 2, 0:n], AX, ALU.max))
                    dve.tensor_scalar(stat[:, 46 + u % 2:47 + u % 2], stat[:, 50 + u % 2:51 + u % 2], -(HD ** -0.5), None,
                                      ALU.mult).then_inc(s_max, 1)
                    for j in range(2 * u, min(2 * u + 2, TAPS)):
                        conv_tap(2, j)
                if u >= 1:
                    w = u - 1
                    n = P if w < QH else 3 * P
                    dve.wait_ge(exp_done, w + 1)
                    link(dve.reciprocal(stat[:, 52 + w % 2:53 + w % 2], stat[:, 48 + w % 2:49 + w % 2]))
                    dve.tensor_scalar(pr[:, w % 2, 0:n], pr[:, w % 2, 0:n], stat[:, 52 + w % 2:53 + w % 2], None,
                                      ALU.mult).then_inc(pr_ready, 1)
            mod_columns(1)
            dve.wait_ge(kv_out, 64)
            for t in range(TT):
                dve.wait_ge(ln_mm, t + 1)
                link(dve.bn_stats(stat[:, 16:22], PS[:, 6 + t % 2, :]))
                dve.bn_aggr(stat[:, 56:58], stat[:, 16:22]).then_inc(ln_var, 1)
                dve.wait_ge(ln_std, t + 1)
                link(dve.reciprocal(stat[:, 60:61], stat[:, 58 + t % 2:59 + t % 2]))
                dve.tensor_scalar(z[:, t, :], PS[:, 6 + t % 2, :], stat[:, 56:57], stat[:, 60:61],
                                  ALU.subtract, ALU.mult).then_inc(z_ready, 1)
            dve.wait_ge(gate_copied, 4)
            for i in range(6):
                t, half = i // 2, i % 2
                s = slice(half * 512, half * 512 + 512)
                dve.wait_ge(out_mm, i + 1)
                part = tm[:, (i % 5) * 512:(i % 5) * 512 + 512]
                link(dve.tensor_tensor(part, PS[:, i, :], gate_row[:, cnd(t), s], ALU.mult))
                i = dve.tensor_tensor(x[:, t, s], x[:, t, s], part, ALU.add)
                if half:
                    i.then_inc(x_ready, 1)
                else:
                    mark(i)

            def experts(l):
                s = 2 * l + 1
                if l == 1:
                    dve.wait_ge(state_out, 32 * RH)
                norm(s)
                t4, t44 = [P, TT, 4], [P, TT, 4, 4]
                row4 = iota4.unsqueeze(1).to_broadcast(t4)

                def wide(i):
                    return rs[:, i, :].unsqueeze(2).to_broadcast(t4)

                def first_max(val, low, hot):
                    link(dve.tensor_scalar(cd, val, 0.0, 8.0, ALU.is_lt, ALU.mult))
                    link(dve.tensor_tensor(cd, cd, row4, ALU.add))
                    link(dve.tensor_reduce(rs[:, low, :], cd, AX, ALU.min))
                    link(dve.tensor_tensor(hot, row4, wide(low), ALU.is_equal))

                dve.wait_ge(router_mm, l + 1)
                link(dve.tensor_tensor(lg, PS[:, 2, 0:60].rearrange("p (a b) -> p a b", a=TT),
                                       V[:, V_RB + 20 * l:V_RB + 20 * l + 20].unsqueeze(1).to_broadcast([P, TT, 20]), ALU.add))
                link(dve.tensor_reduce(rs[:, 0, :], lg[:, :, 0:4], AX, ALU.max))
                dve.tensor_tensor(gd, lg[:, :, 0:4], wide(0), ALU.subtract).then_inc(route_d, 1)
                dve.wait_ge(route_d, 2 * l + 1)
                first_max(gd, 1, oh)
                em4 = em.rearrange("p t (g e) -> p t g e", g=NG)
                link(dve.tensor_tensor(em4, lg[:, :, 4:20].rearrange("p t (g e) -> p t g e", g=NG),
                                       oh.unsqueeze(3).to_broadcast(t44), ALU.mult))
                link(dve.tensor_reduce(es, em.rearrange("p t (g e) -> p t e g", g=NG), AX, ALU.add))
                link(dve.tensor_reduce(rs[:, 2, :], es, AX, ALU.max))
                link(dve.tensor_tensor(ed, es, wide(2), ALU.subtract))
                first_max(ed, 3, o1)
                link(dve.scalar_tensor_tensor(es2, o1, -BIG, es, ALU.mult, ALU.add))
                link(dve.tensor_reduce(rs[:, 4, :], es2, AX, ALU.max))
                dve.tensor_tensor(rs[:, 5, :], rs[:, 4, :], rs[:, 2, :], ALU.subtract).then_inc(route_d, 1)
                link(dve.tensor_tensor(ed, es2, wide(4), ALU.subtract))
                first_max(ed, 3, o2)
                dve.wait_ge(route_e, 2 * l + 2)
                link(dve.tensor_reduce(rs[:, 7, :], ge, AX, ALU.add))
                link(dve.scalar_tensor_tensor(rs[:, 8, :], rs[:, 6, :], 1.0, rs[:, 7, :], ALU.add, ALU.mult))
                link(dve.reciprocal(rs[:, 8, :], rs[:, 8, :]))
                link(dve.tensor_tensor(rs[:, 9, :], rs[:, 6, :], rs[:, 8, :], ALU.mult))
                link(dve.tensor_tensor(cd, o1, o2, ALU.add))
                dve.tensor_tensor(mem.rearrange("p t (g e) -> p t g e", g=NG), oh.unsqueeze(3).to_broadcast(t44),
                                  cd.unsqueeze(2).to_broadcast(t44), ALU.mult).then_inc(mem_ready, 1)
                link(dve.tensor_tensor(ed, o1, wide(8), ALU.mult))
                link(dve.tensor_tensor(es2, o2, wide(9), ALU.mult))
                link(dve.tensor_tensor(ed, ed, es2, ALU.add))
                link(dve.tensor_tensor(comb.rearrange("p t (g e) -> p t g e", g=NG), oh.unsqueeze(3).to_broadcast(t44),
                                       ed.unsqueeze(2).to_broadcast(t44), ALU.mult))
                gate_diag(s)
                dve.wait_ge(rank_mm, l + 1)
                link(dve.scalar_tensor_tensor(key, PS[:, 3, 0:48].rearrange("p (a b) -> p a b", a=TT), 1.0, mem,
                                              ALU.add, ALU.mult))
                link(dve.tensor_scalar(key, key, -1.0, None, ALU.add))
                link(dve.tensor_reduce(cntf, PS[:, 3, 48:64].rearrange("p (a b) -> p a b", b=2), AX, ALU.max))
                dve.tensor_copy(counts, cntf).then_inc(counts_ready, 1)
                dve.wait_ge(counts_ready, l + 1)
                B8, B5 = PAIRS * l, 5 * PAIRS * l
                S0 = (6 * PAIRS + 1) * l + 1
                dve.wait_ge(acc_add, S0)

                def keys_of(dst, src, p):
                    return dve.tensor_copy(dst, src[:, :, bass.ds(2 * p, 2)])

                def select(dst, keys, weights=None):
                    for t in range(TT):
                        for e in range(2):
                            i = dve.tensor_scalar(dst[:, t, CAP * e:CAP * e + CAP], iota_cap, keys[:, t, e:e + 1],
                                                  None if weights is None else weights[:, t, e:e + 1], ALU.is_equal,
                                                  *(() if weights is None else (ALU.mult,)))
                    return i

                def add(p):
                    dve.wait_ge(acc_add, 6 * p + S0)
                    dve.wait_ge(ov_dve, 15 * p + 15 * (B8 + 1))
                    for i in range(6):
                        dve.wait_ge(scat_mm, 6 * p + 6 * B8 + i + 1)
                        s = slice((i % 2) * 512, (i % 2) * 512 + 512)
                        dve.tensor_tensor(acc[:, i // 2, s], acc[:, i // 2, s], PS[:, i % 2, :], ALU.add).then_inc(acc_add, 1)

                K = 7
                K0 = (K * PAIRS + 1) * l

                def pair(p, last_pair=False):
                    n = dve.value_load(counts[0:1, bass.ds(p, 1)], min_val=0, max_val=NT)
                    need(dve, selw_ready, p + B8)
                    need(dve, ov_dve, 15 * p + 15 * B8)
                    keys_of(kB, key, p)
                    keys_of(cB, comb, p).then_inc(pairkey, 1)
                    dve.wait_ge(pairkey, K * p + K0 + 2)
                    need(dve, selT_mm, p + B8)
                    select(selw, kB, cB).then_inc(selw_ready, 1)
                    if not last_pair:
                        dve.wait_ge(sel_ready, p + B8 + 1)
                        keys_of(kA, key, p + 1).then_inc(pairkey, 1)
                        dve.wait_ge(pairkey, K * p + K0 + 3)
                        dve.wait_ge(gath_mm, 2 * p + 2 * (B8 + 1))
                        select(sel, kA).then_inc(sel_ready, 1)
                    else:
                        dve.sem_inc(pairkey, 1)
                    dve.wait_ge(silu_done, p + B8 + 1)
                    dve.wait_ge(eup_mm, p + B8 + 1)
                    dve.tensor_tensor(hid, sgate, PS[:, 1, :], ALU.mult).then_inc(hid_ready, 1)
                    return n

                def tail(p, n, last_pair=False):
                    def unit(step, k):
                        need(dve, ov_dve, 3 * step)
                        dve.tensor_scalar(kB, kB, -float(CAP), None, ALU.add).then_inc(pairkey, 1)
                        dve.wait_ge(pairkey, k)
                        select(sel, kB)
                        select(selw, kB, cB).then_inc(ov_dve, 1)
                        dve.wait_ge(ov_act, 4 * step + 2)
                        dve.tensor_tensor(hid, sgate, PS[:, 1, :], ALU.mult).then_inc(ov_dve, 1)
                        dve.wait_ge(ov_pe, 5 * step + 5)
                        for i, b in enumerate((0, 1, 2, 3, 5, 6)):
                            s = slice((i % 2) * 512, (i % 2) * 512 + 512)
                            w = dve.tensor_tensor(acc[:, i // 2, s], acc[:, i // 2, s], PS[:, b, :], ALU.add)
                        w.then_inc(ov_dve, 1)

                    with dve.If(n > CAP):
                        dve.wait_ge(selw_ready, p + B8 + 1)
                        dve.wait_ge(sel_ready, p + B8 + (1 if last_pair else 2))
                        dve.wait_ge(acc_add, 6 * p + S0)
                        dve.wait_ge(selT_mm, p + B8 + 1)
                        dve.wait_ge(hidT_mm, p + B8 + 1)
                        dve.wait_ge(gath_mm, 2 * p + 2 * (B8 + (1 if last_pair else 2)))
                        unit(5 * p + B5, K * p + K0 + 4)
                        with dve.If(n > 2 * CAP):
                            with dve.Fori(1, UNITS - 1) as u:
                                unit(5 * p + B5 + u, K * p + K0 + 4 + u)
                        with dve.Else():
                            dve.wait_ge(ov_dve, 15 * p + 3 * (B5 + 1))
                            dve.sem_inc(ov_dve, 3 * (UNITS - 2))
                            dve.sem_inc(pairkey, UNITS - 2)
                        dve.nop()
                    with dve.Else():
                        need(dve, ov_dve, 15 * p + 3 * B5)
                        dve.sem_inc(ov_dve, 3 * (UNITS - 1))
                        dve.sem_inc(pairkey, UNITS - 1)
                    dve.nop()

                keys_of(kA, key, 0).then_inc(pairkey, 1)
                dve.wait_ge(pairkey, K0 + 1)
                select(sel, kA).then_inc(sel_ready, 1)
                n = pair(0)
                tail(0, n)
                with dve.Fori(1, PAIRS - 1) as p:
                    n = pair(p)
                    add(p - 1)
                    tail(p, n)
                n = pair(PAIRS - 1, last_pair=True)
                add(PAIRS - 2)
                tail(PAIRS - 1, n, last_pair=True)
                add(PAIRS - 1)
                dve.wait_ge(acc_add, 6 * PAIRS + S0)
                for t in range(TT):
                    link(dve.tensor_tensor(acc[:, t, :], acc[:, t, :], gate_row[:, cnd(t), :], ALU.mult))
                    dve.tensor_tensor(x[:, t, :], x[:, t, :], acc[:, t, :], ALU.add).then_inc(x_ready, 1)

            experts(0)

            norm(2)
            gate_diag(2)
            dve.wait_ge(dec_ready, 1)
            dve.tensor_scalar(dec[:, 4, :], dec[:, 4, :], -1.0, None, ALU.mult).then_inc(dec_ready, 1)
            dve.wait_ge(dec_ready, 3)
            for ev in RET:
                kind, a, b = ev
                if kind == "job" and a[0] in "qk" and b:
                    src = (qtok if a[0] == "q" else ktok)[:, b, :].rearrange("p (a b) -> p a b", a=4)
                    dve.wait_ge(job_copied, COPY_NO[ev])
                    need(dve, rope_done, ROPE_NO[ev] - 1)
                    rope(rtmp[:, 0, :].rearrange("p (a b) -> p a b", a=4), rtmp[:, 1, :].rearrange("p (a b) -> p a b", a=4),
                         src, 4, b).then_inc(rope_done, 1)
                elif kind == "out":
                    t, half = b // 2, b % 2
                    s = slice(half * 512, half * 512 + 512)
                    dve.wait_ge(out_mm, 6 + OUT_NO[ev])
                    if OUT_NO[ev] == 1:
                        dve.wait_ge(gate_copied, 12)
                    need(dve, rope_done, ROPED[ev])
                    dve.tensor_tensor(rtmp[:, 0, :], PS[:, UNTIL[ev] % 3, :], gate_row[:, cnd(t), s],
                                      ALU.mult).then_inc(out_add, 1)
                    dve.wait_ge(out_add, OUT_NO[ev])
                    i = dve.tensor_tensor(x[:, t, s], x[:, t, s], rtmp[:, 0, :], ALU.add)
                    if a == 3 and half:
                        i.then_inc(x_ready, 1)
                        dve.wait_ge(x_ready, 6 + t + 1)
                    else:
                        link(i)
                elif kind == "A":
                    dve.wait_ge(rA_mm, 3 * a + 1)
                    dve.wait_ge(mask_ready, a + 1)
                    need(dve, yr_sq, a)
                    for d in range(2):
                        i = dve.tensor_tensor(smask[:, d, :, :], PS[:, 3, 0:NT].rearrange("p (a b) -> p a b", a=TT),
                                              masks[:, a, d, :].unsqueeze(1).to_broadcast([P, TT, P]), ALU.mult)
                    i.then_inc(smask_ready, 1)
                    dve.wait_ge(rA_mm, 3 * a + 3)
                    dve.wait_ge(st_loaded[a % 2], 32 * (a // 2 + 1))
                    for d in range(2):
                        i = dve.scalar_tensor_tensor(st1[:, d, :], st0[:, a % 2, d, :], dec[:, 2, d * RH + a:d * RH + a + 1],
                                                     PS[:, 5, d * DV:(d + 1) * DV], ALU.mult, ALU.add)
                    i.then_inc(st1_ready, 1)
                elif kind == "B":
                    need(dve, mix_ready, a)
                    for t in range(TT):
                        own, state = ((6, None), (7, 3), (4, 5))[t]
                        dve.wait_ge(rB_mm, TT * a + t + 1)
                        if t == 0:
                            dve.tensor_copy(yr[:, 0].rearrange("p a b -> p (a b)"), PS[:, own, :]).then_inc(yr_ready, 1)
                            continue
                        for d in range(2):
                            c = slice(d * DV, (d + 1) * DV)
                            j = mark(dve.tensor_scalar(yr[:, t, d, :], PS[:, state, c],
                                                       dec[:, 0, d * RH + a:d * RH + a + 1], None, ALU.mult))
                        dve.wait_ge(dve_chain, j)
                        dve.tensor_tensor(yr[:, t].rearrange("p a b -> p (a b)"), yr[:, t].rearrange("p a b -> p (a b)"),
                                          PS[:, own, :], ALU.add).then_inc(yr_ready, 1)
                elif kind == "C":
                    dve.wait_ge(yr_rms, a + 1)
                    link(dve.reciprocal(stat[:, 30:36], stat[:, 24:30]))
                    need(dve, mixT_mm, 2 * a)
                    dve.wait_ge(job_copied, COPY_NO[("job", f"b{a // 2}", 2)])
                    for t in range(TT):
                        for d in range(2):
                            i = dve.scalar_tensor_tensor(yr[:, t, d, :], yr[:, t, d, :], stat[:, 30 + 2 * t + d:31 + 2 * t + d],
                                                         sg1[a // 2 % 2][:, d, t, (a % 2) * DV:(a % 2 + 1) * DV],
                                                         ALU.mult, ALU.mult)
                    link(i)
                    dve.tensor_tensor(mix, yr[:, :, 0, :], yr[:, :, 1, :], ALU.add).then_inc(mix_ready, 1)
            experts(1)
            dve.wait_ge(fg_loaded, 16)
            for t in range(TT):
                dve.wait_ge(rms, 4 * TT + t + 1)
                link(dve.reciprocal(stat[:, 8 + t:9 + t], stat[:, 4 + t:5 + t]))
                dve.scalar_tensor_tensor(h[:, t, :], x[:, t, :], stat[:, 8 + t:9 + t], fg, ALU.mult,
                                         ALU.mult).then_inc(y_ready, 1)


def shape_constants():
    c = np.zeros((P, C_ALL), np.float32)
    i = np.arange(P)
    c[:, C_ID:C_ID + P] = np.eye(P)
    c[:, C_ONE:C_ONE + P] = 1
    c[:, C_IOTA:C_IOTA + CAP] = np.arange(CAP)
    c[:, C_UPPER:C_UPPER + P] = i[:, None] < i[None, :]
    c[:, C_DF:C_DF + P] = np.maximum(i[None, :] - i[:, None], 0)
    c[:, C_DB:C_DB + P] = np.maximum(i[:, None] - i[None, :], 0)
    c[:, C_MF:C_MF + P] = i[None, :] >= i[:, None]
    c[:, C_MB:C_MB + P] = i[:, None] >= i[None, :]
    tok = np.arange(2 * P)
    pos = np.stack([tok // 64, tok % 64]).astype(np.float32)
    freqs = (np.float32(10000.0) ** (-np.arange(32, dtype=np.float32) / np.float32(32))).astype(np.float32)
    ang = pos[:, :, None] * freqs
    cos, sin = np.cos(ang), np.sin(ang)
    for t in range(2):
        for a in range(2):
            for y in range(2):
                o = P * t + 64 * a + 32 * y
                c[:, C_COS + o:C_COS + o + 32] = cos[a, t * P:(t + 1) * P]
                c[:, C_SIN + o:C_SIN + o + 32] = sin[a, t * P:(t + 1) * P] * (-1 if y == 0 else 1)
    for j in range(4):
        c[32 * j, C_SEL2] = 1
        c[32 * j + 1, C_SEL2 + 1] = 1
    c[:, C_IOTA4:C_IOTA4 + 4] = np.arange(4)
    c[:, C_POS] = i + 1
    c[:, C_POS + 1] = P - i
    c[:, C_POS + 2] = P - 1 - i
    c[:, C_POS + 3] = i
    c[:, C_EPS] = EPS
    return c


def kernel(**inputs):
    import numpy as _np
    import concourse.bacc as _bacc
    from concourse import mybir as _mybir
    from concourse.bass_utils import run_bass_kernel_spmd as _run

    a = {k: _np.asarray(v) for k, v in inputs.items()}

    def chunks(v):
        return v.reshape(-1, P).T

    rows = [chunks(a["mod_b0"]), chunks(a["mod_b1"])]
    rows += [chunks(a[n]) for n in ("norm_mix_g0", "norm_ffn_g0", "norm_mix_g1", "norm_ffn_g1",
                                    "conv_b0", "conv_norm_g0", "conv_norm_b0")]
    rows.append(a["conv_w0"].reshape(TAPS, CB, P).transpose(2, 1, 0).reshape(P, CB * TAPS))
    rows.append(_np.stack([a["c_ctx"], a["c"][0]]).reshape(2, KD, P).transpose(2, 1, 0).reshape(P, 2 * KD))
    for l in range(2):
        w = _np.concatenate([a[f"moe_grp_w{l}"], a[f"moe_rtr_w{l}"].transpose(1, 0, 2).reshape(D, NE)], axis=1)
        rows.append(w.reshape(KD, P, 20).transpose(1, 0, 2).reshape(P, KD * 20))
    flat = [_np.concatenate([a[f"moe_grp_b{l}"], a[f"moe_rtr_b{l}"].reshape(-1)]) for l in range(2)]
    flat += [a["ret_decay_fwd1"], a["ret_decay_bwd1"], a["q_norm_g0"], a["k_norm_g0"]]
    rows += [_np.broadcast_to(v, (P, v.size)) for v in flat]

    nc = _bacc.Bacc("TRN2", target_bir_lowering=False, num_devices=1)
    arrays = {}

    def given(name, v):
        arrays[name] = _np.ascontiguousarray(v)
        return nc.dram_tensor(name, v.shape, _mybir.dt.from_np(v.dtype), kind="ExternalInput").ap()

    def made(name, shape):
        return nc.dram_tensor(name, shape, _mybir.dt.from_np(_np.dtype("float32")), kind="ExternalOutput").ap()

    xs = _np.concatenate([a["x_prompt"][0], a["x_sample"][0]])
    args = [given("x_in", xs), given("cst", shape_constants()), given("par", _np.concatenate(rows, axis=1)),
            given("fgain", _np.broadcast_to(a["final_norm_g"], (P, D))),
            given("cache_k", a["cache_k0"][0]), given("cache_v", a["cache_v0"][0]),
            [given("st_f", a["state_ret_fwd1"][0]), given("st_b", a["state_ret_bwd1"][0])]]
    for n in ("mod_w", "in_w", "out_w", "moe_w_gate", "moe_w_up", "moe_w_down"):
        args.append([given(f"{n}{l}", a[f"{n}{l}"]) for l in range(2)])
    args += [made("y_out", (NT, D)), made("new_k", (KH, P, HD)), made("new_v", (KH, P, HD)),
             [made("new_st_f", (RH, DK, DV)), made("new_st_b", (RH, DK, DV))]]
    backbone_kernel(nc, *args)
    r = _run(nc, [arrays], core_ids=[0]).results[0]
    y = r["y_out"]
    return (y[None, 0:P], y[None, P:NT], r["new_k"][None], r["new_v"][None], r["new_st_f"][None], r["new_st_b"][None])
```

```python
from contextlib import ExitStack

import numpy as np

import concourse.bass as bass
from concourse import mybir

F32 = mybir.dt.float32
I32 = mybir.dt.int32
ALU = mybir.AluOpType
ACT = mybir.ActivationFunctionType
AX = mybir.AxisListType.X

P = 128
D = 1024
KD = D // P
TT = 3
NT = TT * P
SLOT = 4096
NSLOT = 6
CONV = 512
CB = CONV // P
TAPS = 31
PAD = TAPS // 2
CTX0 = PAD
LAT0 = PAD + P + PAD + PAD
APAD = LAT0 + 2 * P + PAD
CVN = APAD - 2 * PAD
TOKCOL = [CTX0 - PAD, LAT0 - PAD, LAT0 - PAD + P]
QH, KH, HD = 8, 2, 128
HQK = QH + KH
QPK = QH // KH
RH, DK, DV = 8, 128, 256
NG, EG, NE = 4, 4, 16
PAIRS = NE // 2
FF = 512
CAP = 64
UNITS = NT // CAP
EPS = 1e-6
BIG = 1e30

C_ID, C_ONE, C_IOTA, C_UPPER = 0, 128, 256, 320
C_DF, C_DB, C_MF, C_MB = 448, 576, 704, 832
C_COS, C_SIN = 960, 1216
C_SEL2, C_IOTA4, C_POS, C_EPS, C_SEL20 = 1472, 1474, 1478, 1482, 1484
C_ALL = 1504
V_MODB, V_NG, V_CB, V_CNG, V_CNB, V_CW, V_COND = 0, 96, 128, 132, 136, 140, 264
V_RW, V_RB, V_DEC, V_QKG = 280, 600, 640, 656
V_ALL = 912

STEP_COL = {"q": 0, "k": RH * DK, "v": 2 * RH * DK, "f": 2 * RH * DK + RH * DV, "b": 2 * RH * DK + 2 * RH * DV}


def plan_retention():
    def jobs(*steps):
        return [("job", s, t) for s in steps for t in range(TT)]

    def outs(j, a, b):
        return [("out", j, i) for i in range(a, b)]

    e = jobs("q0", "k0") + [("gate", 0, 0)] + jobs("v0") + [("turn", 0, 0)] + jobs("f0", "b0")
    f = jobs("v1", "f1", "b1")
    e += [("A", 0, 0)] + f[0:2] + [("B", 0, 0)] + f[2:4] + [("A", 1, 0)] + f[4:6] + [("C", 0, 0)] + f[6:7]
    e += [("B", 1, 0)] + f[7:9]
    f = jobs("v2", "f2", "b2")
    e += [("A", 2, 0)] + [("C", 1, 0)] + outs(0, 0, 6) + [("B", 2, 0)] + f[0:2] + [("A", 3, 0)] + f[2:4]
    e += [("C", 2, 0)] + f[4:5] + [("B", 3, 0)] + f[5:9] + [("C", 3, 0)]
    e += jobs("q1", "k1") + [("turn", 1, 0)]
    v, f = jobs("v3"), jobs("f3", "b3")
    e += [("A", 4, 0)] + outs(1, 0, 3) + [("B", 4, 0)] + outs(1, 3, 6) + [("A", 5, 0)] + v[0:1] + [("C", 4, 0)]
    e += v[1:2] + [("B", 5, 0)] + v[2:3] + [("A", 6, 0)] + f[0:1] + [("C", 5, 0)] + f[1:3] + [("B", 6, 0)]
    e += outs(2, 0, 3) + f[3:5] + [("A", 7, 0)] + f[5:6] + outs(2, 3, 6) + [("C", 6, 0)]
    e += [("B", 7, 0)] + [("half", 3, i) for i in range(3)] + [("C", 7, 0)] + outs(3, 0, 6)
    return e


RET = plan_retention()

STREAM, PLACE = [], []


def plan_stream():
    def put(kind, layer, chunks, slots):
        for i, c in enumerate(chunks):
            STREAM.append((kind, layer, c))
            PLACE.append(slots[i % len(slots)])

    first = [("mod", 0, c) for c in range(4)] + [("in", 0, 0), ("in", 0, 1)]
    for c in range(2, 5):
        first += [("in", 0, c)] + [("mod", 0, 3 * c - 2 + i) for i in range(TT) if 3 * c - 2 + i < 12]
    first += [("mod", 1, c) for c in range(12)] + [("out", 0, c) for c in (1, 2, 0)]
    for n, (kind, layer, c) in enumerate(first):
        put(kind, layer, [c], [n % 5])
    put("moe", 0, range(6 * PAIRS), range(6))
    seen = []
    for kind, step, _ in RET:
        key = ("in", 1, step) if kind == "job" else ("out", 1, step) if kind == "out" else None
        if key and key not in seen:
            seen.append(key)
    for n, (kind, layer, c) in enumerate(seen):
        put(kind, layer, [c], [n % 4])
    put("moe", 1, range(6 * PAIRS), range(6))


plan_stream()
INDEX = {key: i for i, key in enumerate(STREAM)}
USES = [sum(PLACE[j] == PLACE[i] for j in range(i)) for i in range(len(STREAM))]
BEFORE = [max([j for j in range(i) if PLACE[j] == PLACE[i]], default=None) for i in range(len(STREAM))]

JOBS = {}
for _c, _k in ((0, CB), (1, CB), (2, TT), (3, TT), (4, TT)):
    for _t in range(_k):
        JOBS[(0, _c, _t)] = len(JOBS) + 1
for _kind, _s, _t in RET:
    if _kind == "job":
        JOBS[(1, _s, _t)] = len(JOBS) + 1
JOBS0 = 2 * CB + 3 * TT
MOD_BANK, MOD_COLS = (6, 1), (5, 0)
NORM_BANK = (0, 4, 4, 4)
SHARED = [e for e in RET if e[0] in ("job", "out")]
ROPES = [e for e in SHARED if e[0] == "job" and e[1][0] in "qk" and e[2] > 0]
UNTIL = {e: n for n, e in enumerate(SHARED)}
COPY_NO = {e: n + 1 for n, e in enumerate([e for e in SHARED if e[0] == "job"])}
OUT_NO = {e: n + 1 for n, e in enumerate([e for e in SHARED if e[0] == "out"])}
ROPE_NO = {e: n + 1 for n, e in enumerate(ROPES)}
ROPED = {e: sum(r in RET[:RET.index(e)] for r in ROPES) for e in SHARED}


def backbone_kernel(nc, x_in, cst, par, fgain, cache_k, cache_v, st_in, mod_w, in_w, out_w, w_gate,
                    w_up, w_down, y_out, new_k, new_v, st_out):
    with ExitStack() as ctx:
        def sb(name, shape, dt=F32):
            return ctx.enter_context(nc.sbuf_tensor(name, shape, dt))[:]

        def sem(name):
            return ctx.enter_context(nc.semaphore(name))

        PS = ctx.enter_context(nc.psum_tensor("PS", [P, 8, 512], F32))

        ring = sb("ring", [P, NSLOT * SLOT])
        x = sb("x", [P, TT, D])
        hT = sb("hT", [P, KD, NT])
        gate_row = sb("gate_row", [P, 2, D])
        C = sb("C", [P, C_ALL])
        V = sb("V", [P, V_ALL])
        cond = sb("cond", [P, KD, 32])
        modc = sb("modc", [P, 2, 48, 2])
        gain = sb("gain", [P, 4, KD, 2])
        stat = sb("stat", [P, 64])
        counts = sb("counts", [P, PAIRS], I32)
        AREA = 17400
        area = sb("area", [P, AREA])

        ident, ones = C[:, C_ID:C_ID + P], C[:, C_ONE:C_ONE + P]
        eps = C[:, C_EPS:C_EPS + 1]
        iota_cap = C[:, C_IOTA:C_IOTA + CAP]
        iota4 = C[:, C_IOTA4:C_IOTA4 + 4]
        junk = gate_row[:, 0, :]

        def slot(i):
            return ring[:, i * SLOT:(i + 1) * SLOT]

        def cutter(*areas):
            left = [[a, 0, n] for a, n in areas]

            def take(*shape):
                n = int(np.prod(shape))
                a = next(a for a in left if a[1] + n <= a[2])
                v = a[0][:, a[1]:a[1] + n]
                a[1] += n
                if len(shape) == 1:
                    return v
                names = "abcd"[:len(shape)]
                return v.rearrange(f"p ({' '.join(names)}) -> p {' '.join(names)}", **dict(zip(names, shape)))
            return take

        m = cutter((area, AREA))
        h, acc, diag_f = m(TT, D), m(TT, D), m(2, KD, P)
        xn = h
        sel, selw, selT, selT_ov = m(TT, P), m(TT, P), m(TT, P), m(TT, P)
        parts = selT
        gT, gT_ov = m(KD, P), m(KD, P)
        sgate, hid, hidT = m(FF), m(FF), m(4, P)
        ysb, y_ov = m(D), m(D)
        fg = m(D)
        lg = m(TT, 20)
        gd, ge, cd, oh, es, es2, o1, o2, ed = (m(TT, 4) for _ in range(9))
        em, mem, comb, key = m(TT, 16), m(TT, 16), m(TT, 16), m(TT, 16)
        rs = m(10, TT)
        cntf = m(PAIRS)
        kA, kB, cB = m(TT, 2), m(TT, 2), m(TT, 2)

        a0 = cutter((area, AREA))
        qk = a0(TT, HQK, HD)
        vv = a0(4, KH, HD)
        kT = a0(KH, 4, P)
        kc = a0(KH, HD)
        cv, apad, tmp2 = a0(CB, CVN), a0(CB, APAD), a0(2, HQK, HD)
        qT, modrow, ctap = a0(QH, NT), a0(2, 512), a0(2, CVN)
        oT = slot(5)[:, 0:QH * NT].rearrange("p (a b) -> p a b", a=QH)
        diag_0 = tmp2.rearrange("p a b c -> p (a b c)")[:, 0:2 * D].rearrange("p (c k j) -> p c k j", c=2, k=KD)
        tm = tmp2.rearrange("p a b c -> p (a b c)")
        sig = tm[:, 0:CB * NT].rearrange("p (a b) -> p a b", a=CB)
        pr = tm[:, 0:3 * NT].rearrange("p (a b) -> p a b", a=3)
        prT = tm[:, 3 * NT:5 * NT].rearrange("p (a b) -> p a b", a=2)
        z = qk.rearrange("p a b c -> p (a b c)")[:, 0:TT * CONV].rearrange("p (a b) -> p a b", a=TT)
        aT = apad.rearrange("p a b -> p (a b)")[:, 0:CB * NT].rearrange("p (a b) -> p a b", a=CB)

        a1 = cutter((area, AREA), (ring[:, 4 * SLOT:6 * SLOT], 2 * SLOT))
        q1T, k1T = a1(4, NT), a1(4, NT)
        ktok, yr, mixT = a1(TT, 512), a1(TT, 2, DV), a1(4, NT)
        qtok = yr.rearrange("p a b c -> p a (b c)")
        masks, kd, smask, mix = a1(RH, 2, P), a1(4, P), a1(2, TT, P), a1(TT, DV)
        smask_v = smask.rearrange("p a b c -> p (a b c)").rearrange("p (a b) -> p a b", a=TT)
        st0, st1, stout, rtmp = a1(2, 2, DV), a1(2, DV), a1(2, DV), a1(2, 512)
        dec = a1(5, 2 * RH)
        v1 = [a1(TT, 512)]
        v1.append(a1(TT, 512))
        sg1 = [a1(2, TT, 512), a1(2, TT, 512)]
        diag_1 = sg1[1].rearrange("p a b c -> p (a b c)")[:, 0:2 * D].rearrange("p (c k j) -> p c k j", c=2, k=KD)
        diags = [diag_0, diag_f, diag_1, diag_f]

        par_loaded, x_loaded, cache_loaded = sem("par_loaded"), [sem(f"x_loaded{t}") for t in range(TT)], sem("cache_loaded")
        ring_loaded = [sem(f"ring_loaded{i}") for i in range(NSLOT)]
        cond_ready, mod_mm, mod_copied, mod_col_mm, mod_ready, gain_ready = map(sem, (
            "cond_ready", "mod_mm", "mod_copied", "mod_col_mm", "mod_ready", "gain_ready"))
        sumsq, rms, xn_ready, xnT_mm, hT_dve, hT_act, x_ready = map(sem, (
            "sumsq", "rms", "xn_ready", "xnT_mm", "hT_dve", "hT_act", "x_ready"))
        diag_ready, gate_mm, gate_copied, proj_mm, out_slot, out_mm, out_add = map(sem, (
            "diag_ready", "gate_mm", "gate_copied", "proj_mm", "out_slot", "out_mm", "out_add"))
        sig_done, glu_done, qk_copied, qk_sq, qk_rms, qk_ready, qkT_mm, qkT_copied = map(sem, (
            "sig_done", "glu_done", "qk_copied", "qk_sq", "qk_rms", "qk_ready", "qkT_mm", "qkT_copied"))
        s_mm, s_max, exp_done, pr_ready, prT_mm, prT_copied, o_mm, o_copied, kv_out = map(sem, (
            "s_mm", "s_max", "exp_done", "pr_ready", "prT_mm", "prT_copied", "o_mm", "o_copied", "kv_out"))
        pad_zero, conv_pool, conv_dve, ln_mm, ln_var, ln_std, z_ready, zT_mm, aT_ready = map(sem, (
            "pad_zero", "conv_pool", "conv_dve", "ln_mm", "ln_var", "ln_std", "z_ready", "zT_mm", "aT_ready"))
        router_part, router_copied = sem("router_part"), sem("router_copied")
        router_mm, route_d, route_e, mem_ready, rank_mm, counts_ready, hback_mm, h_copied = map(sem, (
            "router_mm", "route_d", "route_e", "mem_ready", "rank_mm", "counts_ready", "hback_mm", "h_copied"))
        sums_in_x = sem("sums_in_x")
        pairkey, sel_ready, selw_ready, gath_mm, gath_copied, egate_mm, eup_mm, silu_done, hid_ready = map(sem, (
            "pairkey", "sel_ready", "selw_ready", "gath_mm", "gath_copied", "egate_mm", "eup_mm", "silu_done", "hid_ready"))
        hidT_mm, hidT_copied, selT_mm, selT_copied, down_mm, y_copied, scat_mm, acc_add, = map(sem, (
            "hidT_mm", "hidT_copied", "selT_mm", "selT_copied", "down_mm", "y_copied", "scat_mm", "acc_add"))
        expert_free = [sem("gate_free"), sem("up_free"), sem("down_free")]
        ov_pe, ov_act, ov_dve = sem("ov_pe"), sem("ov_act"), sem("ov_dve")
        dec_ready, mask_exp, mask_ready, job_copied, rope_done, turn_mm, turn_copied = map(sem, (
            "dec_ready", "mask_exp", "mask_ready", "job_copied", "rope_done", "turn_mm", "turn_copied"))
        kd_ready, rA_mm, smask_ready, st1_ready, rB_mm, yr_ready, yr_sq, yr_rms, mix_ready = map(sem, (
            "kd_ready", "rA_mm", "smask_ready", "st1_ready", "rB_mm", "yr_ready", "yr_sq", "yr_rms", "mix_ready"))
        mixT_mm, mixT_copied, stout_ready, state_out = map(sem, ("mixT_mm", "mixT_copied", "stout_ready", "state_out"))
        st_loaded = [sem("st_loaded0"), sem("st_loaded1")]
        y_ready, y_stored, fg_loaded = sem("y_ready"), sem("y_stored"), sem("fg_loaded")
        dve_chain, pool_chain = sem("dve_chain"), sem("pool_chain")

        def need(eng, s, value):
            if not isinstance(value, int) or value > 0:
                eng.wait_ge(s, value)

        def cols(t):
            return slice(t * P, (t + 1) * P)

        def cnd(t):
            return 0 if t == 0 else 1

        def arrived(eng, i):
            eng.wait_ge(ring_loaded[PLACE[i]], 16 * (USES[i] + 1))

        def wslot(i):
            kind, _, c = STREAM[i]
            wide = kind == "out" or (kind == "moe" and c % 6 >= 4)
            return slot(PLACE[i]).rearrange("p (k n) -> p k n", n=D if wide else 512)

        def released(eng, i):
            kind, l, c = STREAM[i]
            if kind == "mod":
                eng.wait_ge(mod_mm, 12 * l + c + 1)
            elif kind == "in":
                eng.wait_ge(proj_mm, JOBS[(l, c, CB - 1 if l == 0 and c < 2 else TT - 1)])
            elif kind == "out" and l == 0:
                s = [1, 2, 0].index(c)
                eng.wait_ge(out_slot if s < 2 else out_mm, s + 1 if s < 2 else 6)
            elif kind == "out":
                eng.wait_ge(out_mm, 6 + OUT_NO[("out", c, 5)])
            else:
                eng.wait_ge(expert_free[c % 6 // 2], PAIRS * l + c // 6 + 1)

        block = ctx.enter_context(nc.Block())

        @block.sync
        def _(sp):
            def fill(i, src):
                sp.dma_start(wslot(i), src).then_inc(ring_loaded[PLACE[i]], 16)

            def free(i):
                if BEFORE[i] is not None:
                    released(sp, BEFORE[i])

            def expert(l, p, j):
                e = 2 * p + j % 2
                w = (w_gate, w_up, w_down)[j // 2][l].rearrange("e (k q) n -> e q k n", q=P)
                return w[e]

            sp.dma_start(V[:, :], par).then_inc(par_loaded, 16)
            sp.dma_start(C[:, :], cst).then_inc(par_loaded, 16)
            for i, (kind, l, c) in enumerate(STREAM):
                if i == 2:
                    for t in range(TT):
                        sp.dma_start(x[:, t, :], x_in[t * P:(t + 1) * P, :]).then_inc(x_loaded[t], 16)
                if kind != "moe":
                    free(i)
                    if kind == "mod":
                        src = mod_w[l][:, c * 512:(c + 1) * 512].rearrange("(k q) n -> q k n", q=P)
                    elif kind == "in":
                        o = c * 512 if l == 0 else STEP_COL[c[0]] + 512 * int(c[1])
                        src = in_w[l][:, o:o + 512].rearrange("(k q) n -> q k n", q=P)
                    else:
                        src = out_w[l][c * 512:(c + 1) * 512, :].rearrange("(k q) n -> q k n", q=P)
                    fill(i, src)
                elif c == 0:
                    for j in range(6):
                        free(i + j)
                        if j == 5 or (l == 1 and j == 4):
                            sp.wait_ge(x_ready, TT * (2 * l + 1))
                        fill(i + j, expert(l, 0, j))
                    with sp.Fori(1, PAIRS) as p:
                        for j in range(6):
                            sp.wait_ge(expert_free[j // 2], p + PAIRS * l)
                            fill(i + j, expert(l, p, j))
            for t in range(TT):
                sp.wait_ge(y_ready, t + 1)
                sp.dma_start(y_out[t * P:(t + 1) * P, :], h[:, t, :]).then_inc(y_stored, 16)
            sp.wait_ge(y_stored, 16 * TT)

        @block.tensor
        def _(pe):
            def modulation(l, chunks):
                def columns(g):
                    pe.wait_ge(mod_copied, g + 1)
                    for i in range(4):
                        o = ((g % 12) * 4 + i) * 2
                        mm = pe.matmul(PS[:, MOD_COLS[l], o:o + 2], modrow[:, g % 2, i * P:(i + 1) * P],
                                       C[:, C_SEL2:C_SEL2 + 2], start=True, stop=True)
                    mm.then_inc(mod_col_mm, 1)

                for c in chunks:
                    g = 12 * l + c
                    i = INDEX[("mod", l, c)]
                    arrived(pe, i)
                    need(pe, mod_copied, g - 1)
                    for kk in range(2):
                        for j in range(4):
                            k = 4 * kk + j
                            mm = pe.matmul(PS[32 * j:32 * j + 32, MOD_BANK[l] + g % 2, :], cond[:, k, :],
                                           wslot(i)[:, k, :], start=kk == 0, stop=kk == 1)
                    mm.then_inc(mod_mm, 1)
                    if c and (l, c) != (0, 4):
                        columns(g - 1)
                if chunks[-1] == 11 or (l, chunks[-1]) == (0, 3):
                    columns(g)

            def norm_turn(s, tiles=range(TT)):
                if s == 1:
                    pe.wait_ge(x_ready, TT)
                for t in tiles:
                    pe.wait_ge(xn_ready, TT * s + t + 1)
                    for half in range(2):
                        if t == 2:
                            pe.wait_ge(hT_act if half else hT_dve, TT * s + 1)
                        for i in range(4):
                            k = 4 * half + i
                            mm = pe.transpose(PS[:, NORM_BANK[s] + 2 * (t % 2) + half, i * P:(i + 1) * P],
                                              xn[:, t, k * P:(k + 1) * P], ident)
                        mm.then_inc(xnT_mm, 1)
                if tiles[-1] == TT - 1:
                    pe.wait_ge(hT_dve, TT * (s + 1))
                    pe.wait_ge(hT_act, TT * (s + 1))

            def gate_rows(s, banks):
                for c in range(2):
                    pe.wait_ge(diag_ready, 2 * s + c + 1)
                    for half in range(2):
                        if len(banks) == 2 and c:
                            pe.wait_ge(gate_copied, 4 * s + half + 1)
                        pe.matmul(PS[:, banks[(2 * c + half) % len(banks)], :], ones,
                                  diags[s][:, c, 4 * half:4 * half + 4, :].rearrange("p a b -> p (a b)"),
                                  start=True, stop=True).then_inc(gate_mm, 1)

            def project(key, lhs, rhs, out, last=KD):
                for k in range(last):
                    mm = pe.matmul(out, lhs(k), rhs(k), start=k == 0, stop=k == last - 1)
                return mm

            pe.wait_ge(cond_ready, 2)
            modulation(0, range(3))
            norm_turn(0, range(2))
            modulation(0, [3])
            norm_turn(0, range(2, 3))
            pe.wait_ge(gain_ready, 1)
            for c in range(2):
                i = INDEX[("in", 0, c)]
                arrived(pe, i)
                for b in range(CB):
                    project(0, lambda k: wslot(i)[:, k, b * P:(b + 1) * P], lambda k: hT[:, k, :],
                            PS[:, 4 * c + b, 0:NT]).then_inc(proj_mm, 1)
            for n in range(3 * TT):
                i = INDEX[("in", 0, 2 + n // TT)]
                arrived(pe, i)
                if n < 3:
                    pe.wait_ge(glu_done, n + 1)
                else:
                    pe.wait_ge(qk_copied, n - 2)
                project(0, lambda k: hT[:, k, cols(n % TT)], lambda k: wslot(i)[:, k, :],
                        PS[:, n % 3, :]).then_inc(proj_mm, 1)
                if n == 0:
                    pe.wait_ge(sig_done, CB)
                if n != 7:
                    modulation(0, [4 + min(n, 7)])
            pe.wait_ge(cache_loaded, 64)
            pe.wait_ge(qk_copied, 3 * TT)
            for n in range(3 * TT):
                c, t = n // TT, n % TT
                pe.wait_ge(qk_ready, n + 1)
                need(pe, qkT_copied, n - 2)
                heads = range(4 * c, 4 * c + 4) if c < 2 else range(QH, HQK)
                for i, hd in enumerate(heads):
                    mm = pe.transpose(PS[:, n % 3, i * P:(i + 1) * P], qk[:, t, hd, :], ident)
                if c == 2 and t == 0:
                    for i in range(KH):
                        mm = pe.transpose(PS[:, n % 3, (KH + i) * P:(KH + i + 1) * P], kc[:, i, :], ident)
                mm.then_inc(qkT_mm, 1)
            pe.wait_ge(glu_done, CB)
            pe.wait_ge(mod_copied, 12)
            gate_rows(0, [3, 4, 5, 6])
            pe.wait_ge(gate_copied, 4)
            pe.wait_ge(qkT_copied, 3 * TT)
            for u in range(TT * QH + 3):
                if u < TT * QH:
                    t, hd = u // QH, u % QH
                    need(pe, exp_done, u - 1)
                    keys = kT[:, hd // QPK, 0:1, :] if t == 0 else kT[:, hd // QPK, 1:4, :]
                    n = P if t == 0 else 3 * P
                    pe.matmul(PS[:, 3 + u % 2, 0:n], qT[:, hd, cols(t)], keys.rearrange("p a b -> p (a b)"),
                              start=True, stop=True).then_inc(s_mm, 1)
                    if u % 2 == 0:
                        modulation(1, [u // 2])
                if 2 <= u < TT * QH + 2:
                    w = u - 2
                    pe.wait_ge(pr_ready, w + 1)
                    need(pe, prT_copied, w - 1)
                    for i in range(1 if w < QH else 3):
                        mm = pe.transpose(PS[:, 5 + w % 2, i * P:(i + 1) * P], pr[:, w % 3, i * P:(i + 1) * P], ident)
                    mm.then_inc(prT_mm, 1)
                if u >= 3:
                    w = u - 3
                    t, hd = w // QH, w % QH
                    pe.wait_ge(prT_copied, w + 1)
                    if w % 4 == 0:
                        need(pe, o_copied, w // 4)
                    tiles = [0] if t == 0 else [1, 2, 3]
                    for i, kt in enumerate(tiles):
                        mm = pe.matmul(PS[:, 7, (w % 4) * P:(w % 4 + 1) * P],
                                       vv[:, kt, hd // QPK, :], prT[:, w % 2, i * P:(i + 1) * P],
                                       start=i == 0, stop=i == len(tiles) - 1)
                    if w % 4 == 3:
                        mm.then_inc(o_mm, 1)
            pe.wait_ge(conv_dve, 1)
            pe.wait_ge(conv_pool, 1)
            pe.wait_ge(o_copied, 2 * TT)
            pe.wait_ge(mod_ready, 3)

            def conv_tokens(t):
                if t == 2:
                    pe.wait_ge(z_ready, 1)
                for b in range(CB):
                    mm = pe.transpose(PS[:, 6 + t % 2, b * P:(b + 1) * P], cv[:, b, TOKCOL[t]:TOKCOL[t] + P], ident)
                mm.then_inc(ln_mm, 1)

            def conv_back(t):
                pe.wait_ge(z_ready, (2, 3, 3)[t])
                if t == 2:
                    pe.wait_ge(aT_ready, 1)
                for b in range(CB):
                    mm = pe.transpose(PS[:, (7, 6, 7)[t], b * P:(b + 1) * P], z[:, t, b * P:(b + 1) * P], ident)
                mm.then_inc(zT_mm, 1)

            def out0(n):
                i = INDEX[("out", 0, (1, 2, 0)[n])]
                arrived(pe, i)
                for t in range(TT):
                    if n == 2:
                        pe.wait_ge(aT_ready, t + 1)
                    for half in range(2):
                        for k in range(4):
                            lhs = aT[:, k, cols(t)] if n == 2 else oT[:, 4 * n + k, cols(t)]
                            mm = pe.matmul(PS[:, 2 * t + half, :], lhs, wslot(i)[:, k, half * 512:half * 512 + 512],
                                           start=n == 0 and k == 0, stop=n == 2 and k == 3)
                        if n == 2:
                            mm.then_inc(out_mm, 1)
                if n < 2:
                    mm.then_inc(out_slot, 1)

            conv_tokens(0)
            conv_tokens(1)
            out0(0)
            conv_tokens(2)
            conv_back(0)
            out0(1)
            conv_back(1)
            conv_back(2)
            out0(2)

            def experts(l):
                s = 2 * l + 1
                norm_turn(s)
                for kk in range(2):
                    for j in range(4):
                        o = V_RW + 160 * l + 20 * (4 * kk + j)
                        mm = pe.matmul(PS[32 * j:32 * j + 32, 1, 0:NT], V[:, o:o + 32], hT[:, 4 * kk + j, :],
                                       start=kk == 0, stop=kk == 1)
                mm.then_inc(router_part, 1)
                pe.wait_ge(router_copied, l + 1)
                for t in range(TT):
                    mm = pe.matmul(PS[:, 2, 20 * t:20 * t + 20], parts[:, t, :], C[:, C_SEL20:C_SEL20 + 20],
                                   start=True, stop=True)
                mm.then_inc(router_mm, 1)
                for t in range(TT):
                    for half in range(2):
                        if t == 2:
                            pe.wait_ge(h_copied, 6 * l + half + 1)
                        for i in range(4):
                            mm = pe.transpose(PS[:, 4 + 2 * (t % 2) + half, i * P:(i + 1) * P],
                                              hT[:, 4 * half + i, cols(t)], ident)
                        mm.then_inc(hback_mm, 1)
                pe.wait_ge(mem_ready, l + 1)
                for t in range(TT):
                    for v in range(t + 1):
                        mm = pe.matmul(PS[:, 3, 16 * t:16 * t + 16], C[:, C_UPPER:C_UPPER + P] if v == t else ones,
                                       mem[:, v, :], start=v == 0, stop=v == t)
                for v in range(TT):
                    mm = pe.matmul(PS[:, 3, 48:64], ones, mem[:, v, :], start=v == 0, stop=v == TT - 1)
                mm.then_inc(rank_mm, 1)
                pe.wait_ge(counts_ready, l + 1)
                pe.wait_ge(h_copied, 6 * l + 6)
                first = INDEX[("moe", l, 0)]
                W = [wslot(first + j) for j in range(6)]
                B8, B5 = PAIRS * l, 5 * PAIRS * l
                S0 = (6 * PAIRS + 1) * l + 1

                def here(p, j):
                    pe.wait_ge(ring_loaded[j], 16 * p + 16 * (USES[first + j] + 1))

                def gather(dst):
                    for half in range(2):
                        for i in range(4):
                            k = 4 * half + i
                            for t in range(TT):
                                mm = pe.matmul(PS[:, 2 + half, i * P:(i + 1) * P], h[:, t, k * P:(k + 1) * P],
                                               sel[:, t, :], start=t == 0, stop=t == TT - 1)
                        if dst:
                            mm.then_inc(gath_mm, 1)
                    return mm

                def up(j, g):
                    for k in range(KD):
                        for e in range(2):
                            mm = pe.matmul(PS[64 * e:64 * e + 64, j, :], g[:, k, 64 * e:64 * e + 64],
                                           W[2 * j + e][:, k, :], start=k == 0, stop=k == KD - 1)
                    return mm

                def hid_turn():
                    for i in range(4):
                        mm = pe.transpose(PS[:, 4, i * P:(i + 1) * P], hid[:, i * P:(i + 1) * P], ident)
                    return mm

                def down(half):
                    for k in range(4):
                        for e in range(2):
                            mm = pe.matmul(PS[64 * e:64 * e + 64, 5 + half, :], hidT[:, k, 64 * e:64 * e + 64],
                                           W[4 + e][:, k, half * 512:half * 512 + 512], start=k == 0, stop=k == 3)
                    return mm

                def scatter(p):
                    pe.wait_ge(y_copied, 2 * p + 2 * (B8 + 1))
                    pe.wait_ge(selT_copied, p + B8 + 1)
                    for i in range(6):
                        if i >= 2:
                            pe.wait_ge(acc_add, 6 * p + S0 + i - 1)
                        pe.matmul(PS[:, i % 2, :], selT[:, i // 2, :], ysb[:, (i % 2) * 512:(i % 2) * 512 + 512],
                                  start=True, stop=True).then_inc(scat_mm, 1)

                def overflow(step):
                    pe.wait_ge(ov_dve, 4 * step + 1)
                    for t in range(TT):
                        pe.transpose(PS[:, 7, t * P:(t + 1) * P], selw[:, t, :], ident)
                    gather(None).then_inc(ov_pe, 1)
                    pe.wait_ge(ov_act, 4 * step + 1)
                    up(0, gT_ov)
                    up(1, gT_ov).then_inc(ov_pe, 1)
                    pe.wait_ge(ov_dve, 4 * step + 2)
                    hid_turn().then_inc(ov_pe, 1)
                    pe.wait_ge(ov_act, 4 * step + 3)
                    down(0)
                    down(1).then_inc(ov_pe, 1)
                    pe.wait_ge(ov_act, 4 * step + 4)
                    for i, b in enumerate((0, 1, 2, 3, 5, 6)):
                        mm = pe.matmul(PS[:, b, :], selT_ov[:, i // 2, :],
                                       y_ov[:, (i % 2) * 512:(i % 2) * 512 + 512], start=True, stop=True)
                    mm.then_inc(ov_pe, 1)
                    pe.wait_ge(ov_dve, 4 * step + 3)

                def pair(p, first_pair=False, last_pair=False):
                    pe.wait_ge(gath_copied, 2 * p + 2 * (B8 + 1))
                    if not first_pair:
                        pe.wait_ge(acc_add, 6 * p + S0 - 6)
                    here(p, 0)
                    here(p, 1)
                    up(0, gT).then_inc(egate_mm, 1)
                    here(p, 2)
                    here(p, 3)
                    up(1, gT).then_inc(eup_mm, 1)
                    if not last_pair:
                        pe.wait_ge(sel_ready, p + B8 + 2)
                        gather(1)
                    else:
                        pe.wait_ge(selw_ready, p + B8 + 1)
                        gate_rows(s, [2, 3])
                    n = pe.value_load(counts[0:1, bass.ds(p, 1)], min_val=0, max_val=NT)
                    pe.wait_ge(hid_ready, p + B8 + 1)
                    hid_turn().then_inc(hidT_mm, 1)
                    if not first_pair:
                        scatter(p - 1)
                    pe.wait_ge(selw_ready, p + B8 + 1)
                    for t in range(TT):
                        mm = pe.transpose(PS[:, 7, t * P:(t + 1) * P], selw[:, t, :], ident)
                    mm.then_inc(selT_mm, 1)
                    pe.wait_ge(hidT_copied, p + B8 + 1)
                    here(p, 4)
                    here(p, 5)
                    for half in range(2):
                        down(half).then_inc(down_mm, 1)
                    with pe.If(n > CAP):
                        if not first_pair:
                            pe.wait_ge(acc_add, 6 * p + S0)
                        pe.wait_ge(gath_copied, 2 * p + 2 * (B8 + (1 if last_pair else 2)))
                        if last_pair:
                            pe.wait_ge(gate_copied, 4 * s + 4)
                        pe.wait_ge(y_copied, 2 * p + 2 * (B8 + 1))
                        pe.wait_ge(selT_copied, p + B8 + 1)
                        overflow(5 * p + B5)
                        with pe.If(n > 2 * CAP):
                            with pe.Fori(1, UNITS - 1) as u:
                                overflow(5 * p + B5 + u)
                        with pe.Else():
                            pe.wait_ge(ov_pe, 25 * p + 5 * (B5 + 1))
                            pe.sem_inc(ov_pe, 5 * (UNITS - 2))
                        pe.nop()
                    with pe.Else():
                        need(pe, ov_pe, 25 * p + 5 * B5)
                        pe.sem_inc(ov_pe, 5 * (UNITS - 1))
                    pe.nop()

                pe.wait_ge(sel_ready, B8 + 1)
                gather(1)
                pair(0, first_pair=True)
                with pe.Fori(1, PAIRS - 1) as p:
                    pair(p)
                pair(PAIRS - 1, last_pair=True)
                pe.wait_ge(acc_add, 6 * (PAIRS - 1) + S0)
                scatter(PAIRS - 1)

            experts(0)

            norm_turn(2)

            def out1(j, part, ks):
                i, t, half = INDEX[("out", 1, j)], part // 2, part % 2
                for k in ks:
                    mm = pe.matmul(PS[:, UNTIL[("out", j, part)] % 3, :], mixT[:, k, cols(t)],
                                   wslot(i)[:, k, half * 512:half * 512 + 512], start=k == 0, stop=k == 3)
                return mm

            for ev in RET:
                kind, a, b = ev
                if kind in ("job", "out"):
                    n = UNTIL[ev]
                    if n >= 3:
                        before = SHARED[n - 3]
                        if before[0] == "job":
                            pe.wait_ge(job_copied, COPY_NO[before])
                        else:
                            pe.wait_ge(out_add, OUT_NO[before])
                if kind == "job":
                    i = INDEX[("in", 1, a)]
                    arrived(pe, i)
                    project(1, lambda k: hT[:, k, cols(b)], lambda k: wslot(i)[:, k, :],
                            PS[:, n % 3, :]).then_inc(proj_mm, 1)
                elif kind == "out":
                    arrived(pe, INDEX[("out", 1, a)])
                    pe.wait_ge(mixT_copied, 2 * (2 * a + 2))
                    out1(a, b, range(2 if ("half", a, b) in RET else 0, 4)).then_inc(out_mm, 1)
                elif kind == "half":
                    n = UNTIL[("out", a, b)]
                    before = SHARED[n - 3]
                    if before[0] == "job":
                        pe.wait_ge(job_copied, COPY_NO[before])
                    else:
                        pe.wait_ge(out_add, OUT_NO[before])
                    arrived(pe, INDEX[("out", 1, a)])
                    pe.wait_ge(mixT_copied, 2 * (2 * a + 1))
                    out1(a, b, range(2))
                elif kind == "gate":
                    gate_rows(2, [3, 4, 5, 6])
                elif kind == "turn":
                    if a == 0:
                        pe.wait_ge(gate_copied, 12)
                    pe.wait_ge(job_copied, COPY_NO[("job", f"k{a}", 2)])
                    pe.wait_ge(rope_done, ROPE_NO[("job", f"k{a}", 2)])
                    for t in range(TT):
                        for j, src in enumerate((qtok, ktok)):
                            need(pe, turn_copied, 6 * a + 2 * t + j - 1 if t else 0)
                            for i in range(4):
                                mm = pe.transpose(PS[:, 3 + j, i * P:(i + 1) * P], src[:, t, i * P:(i + 1) * P], ident)
                            mm.then_inc(turn_mm, 1)
                elif kind == "A":
                    v = v1[a // 2 % 2]
                    o = (a % 2) * DV
                    pe.wait_ge(turn_copied, 6 * (a // 4 + 1))
                    need(pe, yr_ready, TT * a)
                    for t in range(TT):
                        mm = pe.matmul(PS[:, 3, cols(t)], k1T[:, a % 4, cols(t)], q1T[:, a % 4, cols(t)],
                                       start=True, stop=True)
                    mm.then_inc(rA_mm, 1)
                    pe.wait_ge(kd_ready, a + 1)
                    pe.wait_ge(job_copied, COPY_NO[("job", f"v{a // 2}", 2)])
                    for i, t in enumerate((0, 0, 1, 2)):
                        mm = pe.matmul(PS[:, 4 + i // 2, (i % 2) * DV:(i % 2 + 1) * DV], kd[:, i, :], v[:, t, o:o + DV],
                                       start=True, stop=True)
                        if i % 2:
                            mm.then_inc(rA_mm, 1)
                elif kind == "B":
                    v = v1[a // 2 % 2]
                    o = (a % 2) * DV
                    pe.wait_ge(smask_ready, a + 1)
                    need(pe, mixT_copied, 2 * a)
                    pe.wait_ge(st1_ready, a + 1)
                    pe.wait_ge(stout_ready, a + 1)
                    for t in range(TT):
                        own, state = ((6, None), (7, 3), (4, 5))[t]
                        for d in range(2):
                            mm = pe.matmul(PS[:, own, d * DV:(d + 1) * DV], smask[:, d, t, :], v[:, t, o:o + DV],
                                           start=True, stop=True)
                        if t:
                            for d in range(2):
                                s0 = st0[:, a % 2, d, :] if t == 1 + d else st1[:, d, :]
                                mm = pe.matmul(PS[:, state, d * DV:(d + 1) * DV], q1T[:, a % 4, cols(t)], s0,
                                               start=True, stop=True)
                        mm.then_inc(rB_mm, 1)
                elif kind == "C":
                    pe.wait_ge(mix_ready, a + 1)
                    for t in range(TT):
                        for i in range(2):
                            mm = pe.transpose(PS[:, 6 + t // 2, (t % 2 * 2 + i) * P:(t % 2 * 2 + i + 1) * P],
                                              mix[:, t, i * P:(i + 1) * P], ident)
                        if t:
                            mm.then_inc(mixT_mm, 1)
            experts(1)

        @block.scalar
        def _(act):
            def mod_copies(l, chunks):
                for c in chunks:
                    g = 12 * l + c
                    act.wait_ge(mod_mm, g + 1)
                    need(act, mod_col_mm, g - 1)
                    act.activation(modrow[:, g % 2, :], PS[:, MOD_BANK[l] + g % 2, :], ACT.Copy).then_inc(mod_copied, 1)

            def preload(func):
                act.activation(stat[:, 62:63], eps, func)

            def norm_stats(s, t):
                if s and t == 0:
                    preload(ACT.Sqrt)
                if s == 0:
                    act.wait_ge(x_loaded[t], 16)
                else:
                    act.wait_ge(x_ready, TT * (s - 1) + t + 1)
                act.activation(junk, x[:, t, :], ACT.Square, accum_out=stat[:, t:t + 1]).then_inc(sumsq, 1)
                act.wait_ge(sumsq, TT * s + t + 1)
                act.activation(stat[:, 4 + t:5 + t], stat[:, t:t + 1], ACT.Sqrt, bias=eps, scale=1.0 / D).then_inc(rms, 1)

            def norm_evac(s, t):
                l, shift = s // 2, 24 * (s % 2)
                act.wait_ge(xnT_mm, 2 * (TT * s + t) + 2)
                act.wait_ge(gain_ready, (1, 2, 3, 3)[s])
                for i in range(4):
                    k = 4 + i
                    a = act.activation(hT[:, k, cols(t)], PS[:, NORM_BANK[s] + 1 + 2 * (t % 2), i * P:(i + 1) * P], ACT.Identity,
                                       bias=modc[:, l, shift + k, cnd(t):cnd(t) + 1], scale=gain[:, s, k, cnd(t):cnd(t) + 1])
                a.then_inc(hT_act, 1)

            def norm(s):
                for t in range(TT):
                    if s:
                        norm_stats(s, t)
                for t in range(TT):
                    norm_evac(s, t)

            def gate_copies(s, banks):
                for i in range(4):
                    act.wait_ge(gate_mm, 4 * s + i + 1)
                    act.activation(gate_row[:, i // 2, (i % 2) * 512:(i % 2) * 512 + 512],
                                   PS[:, banks[i % len(banks)], :], ACT.Copy).then_inc(gate_copied, 1)

            act.wait_ge(par_loaded, 32)
            act.wait_ge(cond_ready, 1)
            act.activation(cond[:, :, 0:2], V[:, V_COND:V_COND + 16].rearrange("p (k c) -> p k c", c=2),
                           ACT.Silu).then_inc(cond_ready, 1)
            mod_copies(0, range(1))
            for i in range(KH):
                act.dma_start(kc[:, i, :], cache_k[i]).then_inc(cache_loaded, 16)
                act.dma_start(vv[:, 1, i, :], cache_v[i]).then_inc(cache_loaded, 16)
            mod_copies(0, range(1, 2))
            for t in range(TT):
                norm_stats(0, t)
            mod_copies(0, range(2, 4))
            norm(0)
            for b in range(CB):
                act.wait_ge(proj_mm, JOBS[(0, 1, b)])
                act.activation(sig[:, b, :], PS[:, 4 + b, 0:NT], ACT.Sigmoid).then_inc(sig_done, 1)

            def head_rms(n):
                heads = 4 if n < 2 * TT else KH
                act.wait_ge(qk_sq, n + 1)
                act.activation(stat[:, 16 + 4 * (n % 2):16 + 4 * (n % 2) + heads],
                               stat[:, 24 + 4 * (n % 2):24 + 4 * (n % 2) + heads], ACT.Sqrt, bias=eps,
                               scale=1.0 / HD).then_inc(qk_rms, 1)

            for n in range(3 * TT):
                c, t = n // TT, n % TT
                if n == 3 * TT - 1:
                    head_rms(n - 1)
                act.wait_ge(proj_mm, JOBS[(0, 2 + c, t)])
                if c < 2:
                    act.activation(qk[:, t, 4 * c:4 * c + 4, :].rearrange("p a b -> p (a b)"), PS[:, n % 3, :],
                                   ACT.Copy).then_inc(qk_copied, 1)
                else:
                    act.activation(qk[:, t, QH:HQK, :].rearrange("p a b -> p (a b)"), PS[:, n % 3, 0:KH * HD], ACT.Copy)
                    act.activation(vv[:, (0, 2, 3)[t], :, :].rearrange("p a b -> p (a b)"), PS[:, n % 3, KH * HD:512],
                                   ACT.Copy).then_inc(qk_copied, 1)
                if 0 < n < 3 * TT - 1:
                    head_rms(n - 1)
                if n != 7:
                    mod_copies(0, [4 + min(n, 7)])
            head_rms(3 * TT - 1)
            for i in range(KH):
                act.wait_ge(qk_copied, 3 * TT)
                act.dma_start(new_v[i], vv[:, 0, i, :]).then_inc(kv_out, 16)
                act.wait_ge(qk_ready, 2 * TT + 1)
                act.dma_start(new_k[i], qk[:, 0, QH + i, :]).then_inc(kv_out, 16)
            for n in range(3 * TT):
                c, t = n // TT, n % TT
                act.wait_ge(qkT_mm, n + 1)
                if c < 2:
                    a = act.activation(qT[:, 4 * c:4 * c + 4, cols(t)], PS[:, n % 3, :].rearrange("p (a b) -> p a b", a=4),
                                       ACT.Copy)
                else:
                    a = act.activation(kT[:, :, (0, 2, 3)[t], :],
                                       PS[:, n % 3, 0:KH * P].rearrange("p (a b) -> p a b", a=KH), ACT.Copy)
                    if t == 0:
                        a = act.activation(kT[:, :, 1, :], PS[:, n % 3, KH * P:2 * KH * P].rearrange("p (a b) -> p a b", a=KH),
                                           ACT.Copy)
                a.then_inc(qkT_copied, 1)
            preload(ACT.Exp)
            gate_copies(0, [3, 4, 5, 6])
            for u in range(TT * QH + 3):
                if u < TT * QH:
                    n = P if u < QH else 3 * P
                    act.wait_ge(s_max, u + 1)
                    need(act, prT_mm, u - 2)
                    act.activation(pr[:, u % 3, 0:n], PS[:, 3 + u % 2, 0:n], ACT.Exp, bias=stat[:, 46 + u % 2:47 + u % 2],
                                   scale=HD ** -0.5, accum_out=stat[:, 48 + u % 2:49 + u % 2]).then_inc(exp_done, 1)
                    if u % 2 == 0:
                        mod_copies(1, [u // 2])
                if 2 <= u < TT * QH + 2:
                    w = u - 2
                    n = P if w < QH else 3 * P
                    act.wait_ge(prT_mm, w + 1)
                    act.activation(prT[:, w % 2, 0:n], PS[:, 5 + w % 2, 0:n], ACT.Copy).then_inc(prT_copied, 1)
                if u >= 3 and (u - 3) % 4 == 3:
                    g = (u - 3) // 4
                    act.wait_ge(o_mm, g + 1)
                    act.activation(oT[:, 4 * (g % 2):4 * (g % 2) + 4, cols(g // 2)],
                                   PS[:, 7, :].rearrange("p (a b) -> p a b", a=4),
                                   ACT.Copy).then_inc(o_copied, 1)
            for t in range(TT):
                act.wait_ge(ln_var, t + 1)
                act.activation(stat[:, 58 + t % 2:59 + t % 2], stat[:, 57:58], ACT.Sqrt, bias=eps).then_inc(ln_std, 1)
            for t in range(TT):
                act.wait_ge(zT_mm, t + 1)
                for b in range(CB):
                    a = act.activation(aT[:, b, cols(t)], PS[:, (7, 6, 7)[t], b * P:(b + 1) * P], ACT.Silu,
                                       bias=V[:, V_CNB + b:V_CNB + b + 1], scale=V[:, V_CNG + b:V_CNG + b + 1])
                a.then_inc(aT_ready, 1)

            def experts(l):
                s = 2 * l + 1
                norm(s)
                if l == 1:
                    act.dma_start(fg, fgain).then_inc(fg_loaded, 16)
                act.wait_ge(router_part, l + 1)
                act.activation(parts.rearrange("p a b -> p (a b)"), PS[:, 1, 0:NT], ACT.Copy).then_inc(router_copied, 1)
                for i in range(6):
                    act.wait_ge(hback_mm, 6 * l + i + 1)
                    act.activation(h[:, i // 2, (i % 2) * 512:(i % 2) * 512 + 512], PS[:, 4 + i % 4, :],
                                   ACT.Copy).then_inc(h_copied, 1)
                act.wait_ge(route_d, 2 * l + 1)
                act.activation(ge, gd, ACT.Exp).then_inc(route_e, 1)
                act.wait_ge(route_d, 2 * l + 2)
                act.activation(rs[:, 6, :], rs[:, 5, :], ACT.Exp).then_inc(route_e, 1)
                act.wait_ge(counts_ready, l + 1)
                B8, B5 = PAIRS * l, 5 * PAIRS * l
                S0 = (6 * PAIRS + 1) * l + 1

                def copy2(dst, bank):
                    for half in range(2):
                        a = act.activation(dst[:, half * 512:half * 512 + 512], PS[:, bank + half, :], ACT.Copy)
                    return a

                def gathered(p):
                    for half in range(2):
                        act.wait_ge(gath_mm, 2 * p + 2 * B8 + half + 1)
                        act.activation(gT[:, 4 * half:4 * half + 4, :].rearrange("p a b -> p (a b)"), PS[:, 2 + half, :],
                                       ACT.Copy).then_inc(gath_copied, 1)

                def overflow(step, n=None):
                    act.wait_ge(ov_pe, 5 * step + 1)
                    act.activation(selT_ov.rearrange("p a b -> p (a b)"), PS[:, 7, 0:NT], ACT.Copy)
                    copy2(gT_ov.rearrange("p a b -> p (a b)"), 2).then_inc(ov_act, 1)
                    if n is not None:
                        with act.If(n < 2 * CAP + 1):
                            act.wait_ge(ov_pe, 5 * step + 2)
                            act.sem_inc(expert_free[0], 1)
                            act.sem_inc(expert_free[1], 1)
                    act.wait_ge(ov_pe, 5 * step + 2)
                    act.activation(sgate, PS[:, 0, :], ACT.Silu).then_inc(ov_act, 1)
                    act.wait_ge(ov_pe, 5 * step + 3)
                    act.activation(hidT.rearrange("p a b -> p (a b)"), PS[:, 4, :], ACT.Copy).then_inc(ov_act, 1)
                    act.wait_ge(ov_pe, 5 * step + 4)
                    copy2(y_ov, 5).then_inc(ov_act, 1)

                def pair(p, last_pair=False):
                    n = act.value_load(counts[0:1, bass.ds(p, 1)], min_val=0, max_val=NT)
                    act.wait_ge(egate_mm, p + B8 + 1)
                    act.activation(sgate, PS[:, 0, :], ACT.Silu).then_inc(silu_done, 1)
                    with act.If(n < CAP + 1):
                        act.sem_inc(expert_free[0], 1)
                        act.wait_ge(eup_mm, p + B8 + 1)
                        act.sem_inc(expert_free[1], 1)
                    if not last_pair:
                        gathered(p + 1)
                    else:
                        gate_copies(s, [2, 3])
                    act.wait_ge(hidT_mm, p + B8 + 1)
                    act.activation(hidT.rearrange("p a b -> p (a b)"), PS[:, 4, :], ACT.Copy).then_inc(hidT_copied, 1)
                    act.wait_ge(selT_mm, p + B8 + 1)
                    act.activation(selT.rearrange("p a b -> p (a b)"), PS[:, 7, 0:NT], ACT.Copy).then_inc(selT_copied, 1)
                    for half in range(2):
                        act.wait_ge(down_mm, 2 * p + 2 * B8 + half + 1)
                        act.activation(ysb[:, half * 512:half * 512 + 512], PS[:, 5 + half, :],
                                       ACT.Copy).then_inc(y_copied, 1)
                    with act.If(n > CAP):
                        overflow(5 * p + B5, n)
                        with act.If(n > 2 * CAP):
                            with act.Fori(1, UNITS - 1) as u:
                                overflow(5 * p + B5 + u)
                            act.sem_inc(expert_free[0], 1)
                            act.sem_inc(expert_free[1], 1)
                        with act.Else():
                            act.wait_ge(ov_act, 20 * p + 4 * (B5 + 1))
                            act.sem_inc(ov_act, 4 * (UNITS - 2))
                        act.sem_inc(expert_free[2], 1)
                    with act.Else():
                        act.sem_inc(expert_free[2], 1)
                        need(act, ov_act, 20 * p + 4 * B5)
                        act.sem_inc(ov_act, 4 * (UNITS - 1))
                    act.nop()

                gathered(0)
                pair(0)
                with act.Fori(1, PAIRS - 1) as p:
                    pair(p)
                pair(PAIRS - 1, last_pair=True)

            experts(0)

            norm(2)

            def load_state(a):
                for d in range(2):
                    act.dma_start(st0[:, a % 2, d, :], st_in[d][a]).then_inc(st_loaded[a % 2], 16)

            load_state(0)
            load_state(1)
            act.activation(dec[:, 4, :], V[:, V_DEC:V_DEC + 16], ACT.Exp).then_inc(dec_ready, 1)
            act.wait_ge(dec_ready, 2)
            lgam = dec[:, 4, :]
            for d in range(2):
                for h0, pc in ((0, (0, 1)[d]), (1, (2, 3)[d])):
                    act.activation(dec[:, h0, d * RH:(d + 1) * RH], lgam[:, d * RH:(d + 1) * RH], ACT.Exp,
                                   scale=C[:, C_POS + pc:C_POS + pc + 1])
            act.activation(dec[:, 2, :], lgam, ACT.Exp, scale=float(P)).then_inc(dec_ready, 1)
            for a in range(RH):
                for d in range(2):
                    o = (C_DF, C_DB)[d]
                    i = act.activation(masks[:, a, d, :], C[:, o:o + P], ACT.Exp, scale=lgam[:, d * RH + a:d * RH + a + 1])
                i.then_inc(mask_exp, 1)
            for ev in RET:
                kind, a, b = ev
                if kind == "job":
                    act.wait_ge(proj_mm, JOBS[(1, a, b)])
                    bank, part = UNTIL[ev] % 3, int(a[1])
                    if a == "f1" and b == 0:
                        act.wait_ge(gate_mm, 12)
                    if a[0] == "q":
                        need(act, mix_ready, 4 * part)
                        if part == 0:
                            act.wait_ge(gate_copied, 8)
                    dst = {"q": qtok, "k": ktok, "v": v1[part % 2]}.get(a[0])
                    if a[0] in "fb":
                        dst = sg1[part % 2][:, "fb".index(a[0]), :, :]
                        need(act, mix_ready, 2 * (part - 1))
                    if a[0] == "v":
                        need(act, rB_mm, TT * 2 * (part - 1))
                    if a[0] == "k":
                        need(act, kd_ready, 4 * part)
                    act.activation(dst[:, b, :], PS[:, bank, :], ACT.Silu if a[0] in "fb" else ACT.Copy,
                                   scale=DK ** -0.5 if a[0] == "k" else 1.0).then_inc(job_copied, 1)
                elif kind == "gate":
                    gate_copies(2, [3, 4, 5, 6])
                elif kind == "turn":
                    for t in range(TT):
                        for j, dst in enumerate((q1T, k1T)):
                            act.wait_ge(turn_mm, 6 * a + 2 * t + j + 1)
                            act.activation(dst[:, :, cols(t)], PS[:, 3 + j, :].rearrange("p (a b) -> p a b", a=4),
                                           ACT.Copy).then_inc(turn_copied, 1)
                elif kind == "A":
                    act.wait_ge(rA_mm, 3 * a + 2)
                    need(act, state_out, 32 * a)
                    act.activation(stout.rearrange("p a b -> p (a b)"), PS[:, 4, :], ACT.Copy).then_inc(stout_ready, 1)
                    act.wait_ge(stout_ready, a + 1)
                    for d in range(2):
                        act.dma_start(st_out[d][a], stout[:, d, :]).then_inc(state_out, 16)
                elif kind == "B":
                    if a == RH - 1:
                        preload(ACT.Sqrt)
                    act.wait_ge(yr_ready, TT * a + TT)
                    for t in range(TT):
                        for d in range(2):
                            out = (mix, smask_v)[d][:, t, :]
                            i = act.activation(out, yr[:, t, d, :], ACT.Square,
                                               accum_out=stat[:, 16 + 2 * t + d:17 + 2 * t + d])
                    i.then_inc(yr_sq, 1)
                    act.wait_ge(yr_sq, a + 1)
                    act.activation(stat[:, 24:30], stat[:, 16:22], ACT.Sqrt, bias=eps, scale=1.0 / DV).then_inc(yr_rms, 1)
                elif kind == "C":
                    o = 2 * (a % 2)
                    if a % 2 == 0:
                        need(act, out_mm, 6 + 6 * (a // 2) if a else 0)
                    act.wait_ge(mixT_mm, 2 * a + 1)
                    for t in range(2):
                        i = act.activation(mixT[:, o:o + 2, cols(t)],
                                           PS[:, 6, t * 2 * P:(t + 1) * 2 * P].rearrange("p (a b) -> p a b", a=2), ACT.Copy)
                    i.then_inc(mixT_copied, 1)
                    act.wait_ge(mixT_mm, 2 * a + 2)
                    act.activation(mixT[:, o:o + 2, cols(2)], PS[:, 7, 0:2 * P].rearrange("p (a b) -> p a b", a=2),
                                   ACT.Copy).then_inc(mixT_copied, 1)
                    if a + 2 < RH:
                        act.wait_ge(st1_ready, a + 1)
                        load_state(a + 2)
            act.wait_ge(state_out, 32 * RH)
            act.wait_ge(kv_out, 64)
            experts(1)
            for t in range(TT):
                norm_stats(4, t)

        @block.gpsimd
        def _(pool):
            pool.memset(cond, 0.0).then_inc(cond_ready, 1)
            pool.memset(apad, 0.0).then_inc(pad_zero, 1)
            pool.wait_ge(par_loaded, 32)
            pool.wait_ge(glu_done, CB)
            w = V_CW + TAPS * 3
            pool.tensor_scalar(cv[:, 3, :], apad[:, 3, 0:CVN], V[:, w:w + 1], V[:, V_CB + 3:V_CB + 4], ALU.mult,
                               ALU.add).then_inc(pool_chain, 1)
            for j in range(1, TAPS):
                need(pool, pool_chain, 2 * (j - 2) + 1 if j > 2 else 0)
                pool.tensor_scalar(ctap[:, j % 2, :], apad[:, 3, j:j + CVN], V[:, w + j:w + j + 1], None,
                                   ALU.mult).then_inc(pool_chain, 1)
                pool.wait_ge(pool_chain, 2 * j)
                pool.tensor_tensor(cv[:, 3, :], cv[:, 3, :], ctap[:, j % 2, :], ALU.add).then_inc(
                    conv_pool if j == TAPS - 1 else pool_chain, 1)
            pool.wait_ge(x_ready, 3)
            pool.wait_ge(kv_out, 64)
            pool.memset(acc, 0.0).then_inc(acc_add, 1)
            for a in range(RH):
                pool.wait_ge(mask_exp, a + 1)
                i = pool.tensor_tensor(masks[:, a, :, :], masks[:, a, :, :],
                                       C[:, C_MF:C_MF + 2 * P].rearrange("p (a b) -> p a b", a=2), ALU.mult)
                i.then_inc(mask_ready, 1)
            pool.wait_ge(dec_ready, 3)
            for a in range(RH):
                step = f"k{a // 4}"
                pool.wait_ge(job_copied, COPY_NO[("job", step, 2)])
                pool.wait_ge(rope_done, ROPE_NO[("job", step, 2)])
                need(pool, rA_mm, 3 * a)
                for i, (t, d) in enumerate(((0, 0), (0, 1), (1, 0), (2, 1))):
                    o = (a % 4) * P
                    w = pool.tensor_scalar(kd[:, i, :], ktok[:, t, o:o + P], dec[:, 1, d * RH + a:d * RH + a + 1],
                                           None, ALU.mult)
                w.then_inc(kd_ready, 1)
            pool.wait_ge(x_ready, 9)
            pool.wait_ge(state_out, 32 * RH)
            pool.memset(acc, 0.0).then_inc(acc_add, 1)

        @block.vector
        def _(dve):
            links = [0]

            def mark(ins):
                links[0] += 1
                ins.then_inc(dve_chain, 1)
                return links[0]

            def link(ins):
                dve.wait_ge(dve_chain, mark(ins))

            def mod_columns(l, n, a, b, sites):
                dve.wait_ge(mod_col_mm, (4, 12, 24)[n])
                dve.tensor_tensor(modc[:, l, a * KD:b * KD, :],
                                  PS[:, MOD_COLS[l], 2 * a * KD:2 * b * KD].rearrange("p (a b) -> p a b", b=2),
                                  V[:, V_MODB + 48 * l + a * KD:V_MODB + 48 * l + b * KD].unsqueeze(2).to_broadcast(
                                      [P, (b - a) * KD, 2]), ALU.add).then_inc(mod_ready, 1)
                dve.wait_ge(mod_ready, n + 1)
                for s in sites:
                    scale = KD * (1 + 3 * (s % 2))
                    i = dve.scalar_tensor_tensor(gain[:, s, :, :], modc[:, l, scale:scale + KD, :], 1.0,
                                                 V[:, V_NG + 8 * s:V_NG + 8 * s + 8].unsqueeze(2).to_broadcast([P, KD, 2]),
                                                 ALU.add, ALU.mult)
                i.then_inc(gain_ready, 1)
                dve.wait_ge(gain_ready, n + 1)

            def scaled(s, t):
                dve.wait_ge(rms, TT * s + t + 1)
                link(dve.reciprocal(stat[:, 8 + t:9 + t], stat[:, 4 + t:5 + t]))
                if s == 4 and t == 0:
                    dve.wait_ge(fg_loaded, 16)
                if s < 4:
                    dve.tensor_scalar(xn[:, t, :], x[:, t, :], stat[:, 8 + t:9 + t], None, ALU.mult).then_inc(xn_ready, 1)
                else:
                    dve.scalar_tensor_tensor(h[:, t, :], x[:, t, :], stat[:, 8 + t:9 + t], fg, ALU.mult,
                                             ALU.mult).then_inc(y_ready, 1)

            def norm(s, ahead=0):
                l, shift = s // 2, 24 * (s % 2)

                def evac(t):
                    dve.wait_ge(xnT_mm, 2 * (TT * s + t) + 1)
                    for k in range(4):
                        i = dve.tensor_scalar(hT[:, k, cols(t)], PS[:, NORM_BANK[s] + 2 * (t % 2), k * P:(k + 1) * P],
                                              gain[:, s, k, cnd(t):cnd(t) + 1], modc[:, l, shift + k, cnd(t):cnd(t) + 1],
                                              ALU.mult, ALU.add)
                    i.then_inc(hT_dve, 1)

                for t in range(ahead, 2):
                    scaled(s, t)
                if s == 0:
                    scaled(s, 2)
                    mod_columns(0, 0, 0, 2, [0])
                evac(0)
                if s:
                    scaled(s, 2)
                evac(1)
                evac(2)

            def gate_diag(s):
                l, piece = s // 2, 16 + 24 * (s % 2)
                for c in range(2):
                    dve.tensor_tensor(diags[s][:, c, :, :], ident.unsqueeze(1).to_broadcast([P, KD, P]),
                                      modc[:, l, piece:piece + KD, c].unsqueeze(2).to_broadcast([P, KD, P]),
                                      ALU.mult).then_inc(diag_ready, 1)

            def rope(a, b, src, heads, t):
                cos = C[:, C_COS + P * (t - 1):C_COS + P * t].unsqueeze(1).to_broadcast([P, heads, P])
                sin = C[:, C_SIN + P * (t - 1):C_SIN + P * t].rearrange("p (x y j) -> p x y j", x=2, y=2)
                dve.tensor_tensor(a, src, cos, ALU.mult)
                for x in range(2):
                    s4 = src[:, :, 64 * x:64 * x + 64].rearrange("p h (y j) -> p h y j", y=2)
                    b4 = b[:, :, 64 * x:64 * x + 64].rearrange("p h (y j) -> p h y j", y=2)
                    for y in range(2):
                        i = dve.tensor_tensor(b4[:, :, y, :], s4[:, :, 1 - y, :],
                                              sin[:, x, y, :].unsqueeze(1).to_broadcast([P, heads, 32]), ALU.mult)
                link(i)
                return dve.tensor_tensor(src, a, b, ALU.add)

            dve.wait_ge(par_loaded, 32)
            norm(0)
            dve.wait_ge(pad_zero, 1)
            for b in range(CB):
                dve.wait_ge(sig_done, b + 1)
                dve.wait_ge(proj_mm, JOBS[(0, 0, b)])
                dve.tensor_tensor(apad[:, b, CTX0:CTX0 + P], PS[:, b, 0:P], sig[:, b, 0:P], ALU.mult)
                dve.tensor_tensor(apad[:, b, LAT0:LAT0 + 2 * P], PS[:, b, P:NT], sig[:, b, P:NT],
                                  ALU.mult).then_inc(glu_done, 1)
            last = [None] * 3

            def conv_tap(b, j):
                o = V_CW + TAPS * b + j
                if j == 0:
                    i = dve.tensor_scalar(cv[:, b, :], apad[:, b, 0:CVN], V[:, o:o + 1], V[:, V_CB + b:V_CB + b + 1],
                                          ALU.mult, ALU.add)
                else:
                    dve.wait_ge(dve_chain, last[b])
                    i = dve.scalar_tensor_tensor(cv[:, b, :], apad[:, b, j:j + CVN], V[:, o:o + 1], cv[:, b, :],
                                                 ALU.mult, ALU.add)
                if b == 2 and j == TAPS - 1:
                    i.then_inc(conv_dve, 1)
                else:
                    last[b] = mark(i)

            dve.wait_ge(glu_done, 3)
            taps = [(b, j) for j in range(TAPS) for b in range(2)]
            early = 3 * TAPS - 2 * (TT * QH + 1)
            for n in range(3 * TT):
                c, t = n // TT, n % TT
                hs = slice(4 * c, 4 * c + 4) if c < 2 else slice(QH, HQK)
                heads = 4 if c < 2 else KH
                g = V_QKG + (0 if c < 2 else HD)
                r = stat[:, 16 + 4 * (n % 2):16 + 4 * (n % 2) + heads]
                ta, tb = (tm[:, 1024 * (n % 2) + 512 * i:1024 * (n % 2) + 512 * i + heads * HD].rearrange(
                    "p (a b) -> p a b", a=heads) for i in range(2))
                dve.wait_ge(qk_copied, n + 1)
                need(dve, qk_ready, n - 1)
                link(dve.tensor_tensor(ta, qk[:, t, hs], qk[:, t, hs], ALU.mult))
                dve.tensor_reduce(stat[:, 24 + 4 * (n % 2):24 + 4 * (n % 2) + heads], ta, AX, ALU.add).then_inc(qk_sq, 1)
                for b, j in taps[5 * n:min(5 * n + 5, early)]:
                    conv_tap(b, j)
                dve.wait_ge(qk_rms, n + 1)
                link(dve.reciprocal(r, r))
                link(dve.tensor_tensor(qk[:, t, hs], qk[:, t, hs], r.unsqueeze(2).to_broadcast([P, heads, HD]), ALU.mult))
                i = dve.tensor_tensor(qk[:, t, hs], qk[:, t, hs], V[:, g:g + HD].unsqueeze(1).to_broadcast([P, heads, HD]),
                                      ALU.mult)
                if t:
                    link(i)
                    i = rope(ta, tb, qk[:, t, hs], heads, t)
                i.then_inc(qk_ready, 1)
            mod_columns(0, 1, 2, 6, [1])
            dve.wait_ge(qk_ready, 3 * TT)
            gate_diag(0)
            first, block2 = taps[early:], [(2, j) for j in range(TAPS)]
            taps = [tap for pair in zip(first, block2) for tap in pair] + block2[len(first):]
            for u in range(TT * QH + 1):
                if u < TT * QH:
                    n = P if u < QH else 3 * P
                    dve.wait_ge(s_mm, u + 1)
                    link(dve.tensor_reduce(stat[:, 50 + u % 2:51 + u % 2], PS[:, 3 + u % 2, 0:n], AX, ALU.max))
                    dve.tensor_scalar(stat[:, 46 + u % 2:47 + u % 2], stat[:, 50 + u % 2:51 + u % 2], -(HD ** -0.5), None,
                                      ALU.mult).then_inc(s_max, 1)
                if u >= 1:
                    w = u - 1
                    n = P if w < QH else 3 * P
                    dve.wait_ge(exp_done, w + 1)
                    link(dve.reciprocal(stat[:, 52 + w % 2:53 + w % 2], stat[:, 48 + w % 2:49 + w % 2]))
                    dve.tensor_scalar(pr[:, w % 3, 0:n], pr[:, w % 3, 0:n], stat[:, 52 + w % 2:53 + w % 2], None,
                                      ALU.mult).then_inc(pr_ready, 1)
                for b, j in taps[2 * u:2 * u + 2]:
                    conv_tap(b, j)
            mod_columns(1, 2, 0, 6, [2, 3])
            dve.wait_ge(kv_out, 64)
            for t in range(TT):
                dve.wait_ge(ln_mm, t + 1)
                link(dve.bn_stats(stat[:, 16:22], PS[:, 6 + t % 2, :]))
                dve.bn_aggr(stat[:, 56:58], stat[:, 16:22]).then_inc(ln_var, 1)
                dve.wait_ge(ln_std, t + 1)
                link(dve.reciprocal(stat[:, 60:61], stat[:, 58 + t % 2:59 + t % 2]))
                dve.tensor_scalar(z[:, t, :], PS[:, 6 + t % 2, :], stat[:, 56:57], stat[:, 60:61],
                                  ALU.subtract, ALU.mult).then_inc(z_ready, 1)
            dve.wait_ge(gate_copied, 4)
            for i in range(6):
                t, half = i // 2, i % 2
                s = slice(half * 512, half * 512 + 512)
                dve.wait_ge(out_mm, i + 1)
                part = tm[:, (i % 5) * 512:(i % 5) * 512 + 512]
                link(dve.tensor_tensor(part, PS[:, i, :], gate_row[:, cnd(t), s], ALU.mult))
                i = dve.tensor_tensor(x[:, t, s], x[:, t, s], part, ALU.add)
                if half:
                    i.then_inc(x_ready, 1)
                else:
                    mark(i)

            def experts(l):
                s = 2 * l + 1
                norm(s, l)
                t4, t44 = [P, TT, 4], [P, TT, 4, 4]
                row4 = iota4.unsqueeze(1).to_broadcast(t4)

                def wide(i):
                    return rs[:, i, :].unsqueeze(2).to_broadcast(t4)

                def first_max(val, low, hot):
                    link(dve.tensor_scalar(cd, val, 0.0, 8.0, ALU.is_lt, ALU.mult))
                    link(dve.tensor_tensor(cd, cd, row4, ALU.add))
                    link(dve.tensor_reduce(rs[:, low, :], cd, AX, ALU.min))
                    link(dve.tensor_tensor(hot, row4, wide(low), ALU.is_equal))

                dve.wait_ge(router_mm, l + 1)
                link(dve.tensor_tensor(lg, PS[:, 2, 0:60].rearrange("p (a b) -> p a b", a=TT),
                                       V[:, V_RB + 20 * l:V_RB + 20 * l + 20].unsqueeze(1).to_broadcast([P, TT, 20]), ALU.add))
                link(dve.tensor_reduce(rs[:, 0, :], lg[:, :, 0:4], AX, ALU.max))
                dve.tensor_tensor(gd, lg[:, :, 0:4], wide(0), ALU.subtract).then_inc(route_d, 1)
                dve.wait_ge(route_d, 2 * l + 1)
                first_max(gd, 1, oh)
                em4 = em.rearrange("p t (g e) -> p t g e", g=NG)
                link(dve.tensor_tensor(em4, lg[:, :, 4:20].rearrange("p t (g e) -> p t g e", g=NG),
                                       oh.unsqueeze(3).to_broadcast(t44), ALU.mult))
                link(dve.tensor_reduce(es, em.rearrange("p t (g e) -> p t e g", g=NG), AX, ALU.add))
                link(dve.tensor_reduce(rs[:, 2, :], es, AX, ALU.max))
                link(dve.tensor_tensor(ed, es, wide(2), ALU.subtract))
                first_max(ed, 3, o1)
                link(dve.scalar_tensor_tensor(es2, o1, -BIG, es, ALU.mult, ALU.add))
                link(dve.tensor_reduce(rs[:, 4, :], es2, AX, ALU.max))
                dve.tensor_tensor(rs[:, 5, :], rs[:, 4, :], rs[:, 2, :], ALU.subtract).then_inc(route_d, 1)
                link(dve.tensor_tensor(ed, es2, wide(4), ALU.subtract))
                first_max(ed, 3, o2)
                link(dve.tensor_tensor(cd, o1, o2, ALU.add))
                dve.tensor_tensor(mem.rearrange("p t (g e) -> p t g e", g=NG), oh.unsqueeze(3).to_broadcast(t44),
                                  cd.unsqueeze(2).to_broadcast(t44), ALU.mult).then_inc(mem_ready, 1)
                dve.wait_ge(route_e, 2 * l + 2)
                link(dve.tensor_reduce(rs[:, 7, :], ge, AX, ALU.add))
                link(dve.scalar_tensor_tensor(rs[:, 8, :], rs[:, 6, :], 1.0, rs[:, 7, :], ALU.add, ALU.mult))
                link(dve.reciprocal(rs[:, 8, :], rs[:, 8, :]))
                link(dve.tensor_tensor(rs[:, 9, :], rs[:, 6, :], rs[:, 8, :], ALU.mult))
                link(dve.tensor_tensor(ed, o1, wide(8), ALU.mult))
                link(dve.tensor_tensor(es2, o2, wide(9), ALU.mult))
                link(dve.tensor_tensor(ed, ed, es2, ALU.add))
                link(dve.tensor_tensor(comb.rearrange("p t (g e) -> p t g e", g=NG), oh.unsqueeze(3).to_broadcast(t44),
                                       ed.unsqueeze(2).to_broadcast(t44), ALU.mult))
                dve.wait_ge(rank_mm, l + 1)
                link(dve.scalar_tensor_tensor(key, PS[:, 3, 0:48].rearrange("p (a b) -> p a b", a=TT), 1.0, mem,
                                              ALU.add, ALU.mult))
                link(dve.tensor_scalar(key, key, -1.0, None, ALU.add))
                link(dve.tensor_reduce(cntf, PS[:, 3, 48:64].rearrange("p (a b) -> p a b", b=2), AX, ALU.max))
                dve.tensor_copy(counts, cntf).then_inc(counts_ready, 1)
                dve.wait_ge(counts_ready, l + 1)
                B8, B5 = PAIRS * l, 5 * PAIRS * l
                S0 = (6 * PAIRS + 1) * l + 1
                dve.wait_ge(acc_add, S0)

                def keys_of(dst, src, p):
                    return dve.tensor_copy(dst, src[:, :, bass.ds(2 * p, 2)])

                def select(dst, keys, weights=None):
                    for t in range(TT):
                        for e in range(2):
                            i = dve.tensor_scalar(dst[:, t, CAP * e:CAP * e + CAP], iota_cap, keys[:, t, e:e + 1],
                                                  None if weights is None else weights[:, t, e:e + 1], ALU.is_equal,
                                                  *(() if weights is None else (ALU.mult,)))
                    return i

                def add(p):
                    dve.wait_ge(acc_add, 6 * p + S0)
                    dve.wait_ge(ov_dve, 20 * p + 20 * (B8 + 1))
                    for i in range(6):
                        dve.wait_ge(scat_mm, 6 * p + 6 * B8 + i + 1)
                        s = slice((i % 2) * 512, (i % 2) * 512 + 512)
                        dve.tensor_tensor(acc[:, i // 2, s], acc[:, i // 2, s], PS[:, i % 2, :], ALU.add).then_inc(acc_add, 1)

                K = 7
                K0 = (K * PAIRS + 1 + UNITS - 1) * l

                def pair(p, last_pair=False):
                    n = dve.value_load(counts[0:1, bass.ds(p, 1)], min_val=0, max_val=NT)
                    need(dve, selw_ready, p + B8)
                    need(dve, ov_dve, 20 * p + 20 * B8)
                    keys_of(kB, key, p)
                    keys_of(cB, comb, p).then_inc(pairkey, 1)
                    dve.wait_ge(pairkey, K * p + K0 + 2)
                    need(dve, selT_mm, p + B8)
                    select(selw, kB, cB).then_inc(selw_ready, 1)
                    if not last_pair:
                        dve.wait_ge(sel_ready, p + B8 + 1)
                        keys_of(kA, key, p + 1).then_inc(pairkey, 1)
                        dve.wait_ge(pairkey, K * p + K0 + 3)
                        dve.wait_ge(gath_mm, 2 * p + 2 * (B8 + 1))
                        select(sel, kA).then_inc(sel_ready, 1)
                    else:
                        dve.sem_inc(pairkey, 1)
                    dve.wait_ge(silu_done, p + B8 + 1)
                    dve.wait_ge(eup_mm, p + B8 + 1)
                    dve.tensor_tensor(hid, sgate, PS[:, 1, :], ALU.mult).then_inc(hid_ready, 1)
                    return n

                def sums_to_x():
                    dve.wait_ge(acc_add, 6 * (PAIRS - 1) + S0)
                    dve.wait_ge(gate_copied, 4 * s + 4)
                    for t in range(TT):
                        i = dve.tensor_tensor(acc[:, t, :], acc[:, t, :], gate_row[:, cnd(t), :], ALU.mult)
                    i.then_inc(sums_in_x, 1)
                    dve.wait_ge(sums_in_x, 2 * l + 1)
                    for t in range(TT):
                        i = dve.tensor_tensor(x[:, t, :], x[:, t, :], acc[:, t, :], ALU.add)
                    i.then_inc(sums_in_x, 1)
                    dve.wait_ge(sums_in_x, 2 * l + 2)

                def tail(p, n, last_pair=False):
                    def unit(step, k, first=False):
                        need(dve, ov_dve, 4 * step)
                        dve.tensor_scalar(kB, kB, -float(CAP), None, ALU.add).then_inc(pairkey, 1)
                        dve.wait_ge(pairkey, k)
                        select(sel, kB)
                        select(selw, kB, cB).then_inc(ov_dve, 1)
                        if first and last_pair:
                            sums_to_x()
                        dve.wait_ge(ov_act, 4 * step + 2)
                        dve.tensor_tensor(hid, sgate, PS[:, 1, :], ALU.mult).then_inc(ov_dve, 1)
                        dve.wait_ge(ov_pe, 5 * step + 5)
                        for i, b in enumerate((0, 1, 2, 3, 5, 6)):
                            c = slice((i % 2) * 512, (i % 2) * 512 + 512)
                            if last_pair:
                                w = dve.tensor_tensor(acc[:, i // 2, c], PS[:, b, :], gate_row[:, cnd(i // 2), c], ALU.mult)
                            else:
                                w = dve.tensor_tensor(acc[:, i // 2, c], acc[:, i // 2, c], PS[:, b, :], ALU.add)
                            if i in (1, 5):
                                w.then_inc(ov_dve, 1)
                        if last_pair:
                            dve.wait_ge(ov_dve, 4 * step + 4)
                            dve.tensor_tensor(x, x, acc, ALU.add).then_inc(pairkey, 1)
                            dve.wait_ge(pairkey, k + 1)

                    per_unit = 2 if last_pair else 1
                    with dve.If(n > CAP):
                        dve.wait_ge(selw_ready, p + B8 + 1)
                        dve.wait_ge(sel_ready, p + B8 + (1 if last_pair else 2))
                        dve.wait_ge(acc_add, 6 * p + S0)
                        dve.wait_ge(selT_mm, p + B8 + 1)
                        dve.wait_ge(hidT_mm, p + B8 + 1)
                        dve.wait_ge(gath_mm, 2 * p + 2 * (B8 + (1 if last_pair else 2)))
                        unit(5 * p + B5, K * p + K0 + 4, first=True)
                        with dve.If(n > 2 * CAP):
                            with dve.Fori(1, UNITS - 1) as u:
                                unit(5 * p + B5 + u, u * per_unit + (K * p + K0 + 4))
                        with dve.Else():
                            dve.wait_ge(ov_dve, 20 * p + 4 * (B5 + 1))
                            dve.sem_inc(ov_dve, 4 * (UNITS - 2))
                            dve.sem_inc(pairkey, per_unit * (UNITS - 2))
                        dve.nop()
                    with dve.Else():
                        if last_pair:
                            sums_to_x()
                        need(dve, ov_dve, 20 * p + 4 * B5)
                        dve.sem_inc(ov_dve, 4 * (UNITS - 1))
                        dve.sem_inc(pairkey, per_unit * (UNITS - 1))
                    dve.nop()

                keys_of(kA, key, 0).then_inc(pairkey, 1)
                dve.wait_ge(pairkey, K0 + 1)
                select(sel, kA).then_inc(sel_ready, 1)
                gate_diag(s)
                n = pair(0)
                tail(0, n)
                with dve.Fori(1, PAIRS - 1) as p:
                    n = pair(p)
                    add(p - 1)
                    tail(p, n)
                n = pair(PAIRS - 1, last_pair=True)
                add(PAIRS - 2)
                tail(PAIRS - 1, n, last_pair=True)
                dve.wait_ge(ov_dve, 20 * (B8 + PAIRS))
                for i in range(6):
                    t, c = i // 2, slice((i % 2) * 512, (i % 2) * 512 + 512)
                    dve.wait_ge(scat_mm, 6 * (PAIRS - 1 + B8) + i + 1)
                    dve.tensor_tensor(acc[:, t, c], PS[:, i % 2, :], gate_row[:, cnd(t), c], ALU.mult).then_inc(acc_add, 1)
                    dve.wait_ge(acc_add, 6 * (PAIRS - 1) + S0 + i + 1)
                    w = dve.tensor_tensor(x[:, t, c], x[:, t, c], acc[:, t, c], ALU.add)
                    if i % 2:
                        w.then_inc(x_ready, 1)
                    else:
                        mark(w)
                    if i == 3:
                        scaled(s + 1, 0)

            experts(0)

            norm(2, 1)
            gate_diag(2)
            dve.wait_ge(dec_ready, 1)
            dve.tensor_scalar(dec[:, 4, :], dec[:, 4, :], -1.0, None, ALU.mult).then_inc(dec_ready, 1)
            dve.wait_ge(dec_ready, 3)
            order = [e for e in RET if e != ("C", 6, 0)]
            order.insert(order.index(("out", 2, 3)), ("C", 6, 0))
            for ev in order:
                kind, a, b = ev
                if kind == "job" and a[0] in "qk" and b:
                    src = (qtok if a[0] == "q" else ktok)[:, b, :].rearrange("p (a b) -> p a b", a=4)
                    dve.wait_ge(job_copied, COPY_NO[ev])
                    need(dve, rope_done, ROPE_NO[ev] - 1)
                    rope(rtmp[:, 0, :].rearrange("p (a b) -> p a b", a=4), rtmp[:, 1, :].rearrange("p (a b) -> p a b", a=4),
                         src, 4, b).then_inc(rope_done, 1)
                elif kind == "out":
                    t, half = b // 2, b % 2
                    s = slice(half * 512, half * 512 + 512)
                    dve.wait_ge(out_mm, 6 + OUT_NO[ev])
                    if OUT_NO[ev] == 1:
                        dve.wait_ge(gate_copied, 12)
                    need(dve, rope_done, ROPED[ev])
                    dve.tensor_tensor(rtmp[:, 0, :], PS[:, UNTIL[ev] % 3, :], gate_row[:, cnd(t), s],
                                      ALU.mult).then_inc(out_add, 1)
                    dve.wait_ge(out_add, OUT_NO[ev])
                    i = dve.tensor_tensor(x[:, t, s], x[:, t, s], rtmp[:, 0, :], ALU.add)
                    if a == 3 and half:
                        i.then_inc(x_ready, 1)
                        dve.wait_ge(x_ready, 6 + t + 1)
                        if t == 1:
                            dve.wait_ge(state_out, 32 * RH)
                            scaled(3, 0)
                    else:
                        link(i)
                elif kind == "A":
                    dve.wait_ge(rA_mm, 3 * a + 1)
                    dve.wait_ge(mask_ready, a + 1)
                    need(dve, yr_sq, a)
                    for d in range(2):
                        i = dve.tensor_tensor(smask[:, d, :, :], PS[:, 3, 0:NT].rearrange("p (a b) -> p a b", a=TT),
                                              masks[:, a, d, :].unsqueeze(1).to_broadcast([P, TT, P]), ALU.mult)
                    i.then_inc(smask_ready, 1)
                    dve.wait_ge(rA_mm, 3 * a + 3)
                    dve.wait_ge(st_loaded[a % 2], 32 * (a // 2 + 1))
                    for d in range(2):
                        i = dve.scalar_tensor_tensor(st1[:, d, :], st0[:, a % 2, d, :], dec[:, 2, d * RH + a:d * RH + a + 1],
                                                     PS[:, 5, d * DV:(d + 1) * DV], ALU.mult, ALU.add)
                    i.then_inc(st1_ready, 1)
                elif kind == "B":
                    need(dve, mix_ready, a)
                    for t in range(TT):
                        own, state = ((6, None), (7, 3), (4, 5))[t]
                        dve.wait_ge(rB_mm, TT * a + t + 1)
                        if t == 0:
                            dve.tensor_copy(yr[:, 0].rearrange("p a b -> p (a b)"), PS[:, own, :]).then_inc(yr_ready, 1)
                            continue
                        for d in range(2):
                            c = slice(d * DV, (d + 1) * DV)
                            j = mark(dve.tensor_scalar(yr[:, t, d, :], PS[:, state, c],
                                                       dec[:, 0, d * RH + a:d * RH + a + 1], None, ALU.mult))
                        dve.wait_ge(dve_chain, j)
                        dve.tensor_tensor(yr[:, t].rearrange("p a b -> p (a b)"), yr[:, t].rearrange("p a b -> p (a b)"),
                                          PS[:, own, :], ALU.add).then_inc(yr_ready, 1)
                elif kind == "C":
                    dve.wait_ge(yr_rms, a + 1)
                    link(dve.reciprocal(stat[:, 30:36], stat[:, 24:30]))
                    need(dve, mixT_mm, 2 * a)
                    dve.wait_ge(job_copied, COPY_NO[("job", f"b{a // 2}", 2)])
                    for t in range(TT):
                        for d in range(2):
                            i = dve.scalar_tensor_tensor(yr[:, t, d, :], yr[:, t, d, :], stat[:, 30 + 2 * t + d:31 + 2 * t + d],
                                                         sg1[a // 2 % 2][:, d, t, (a % 2) * DV:(a % 2 + 1) * DV],
                                                         ALU.mult, ALU.mult)
                    link(i)
                    dve.tensor_tensor(mix, yr[:, :, 0, :], yr[:, :, 1, :], ALU.add).then_inc(mix_ready, 1)
            experts(1)
            scaled(4, 1)
            scaled(4, 2)


def shape_constants():
    c = np.zeros((P, C_ALL), np.float32)
    i = np.arange(P)
    c[:, C_ID:C_ID + P] = np.eye(P)
    c[:, C_ONE:C_ONE + P] = 1
    c[:, C_IOTA:C_IOTA + CAP] = np.arange(CAP)
    c[:, C_UPPER:C_UPPER + P] = i[:, None] < i[None, :]
    c[:, C_DF:C_DF + P] = np.maximum(i[None, :] - i[:, None], 0)
    c[:, C_DB:C_DB + P] = np.maximum(i[:, None] - i[None, :], 0)
    c[:, C_MF:C_MF + P] = i[None, :] >= i[:, None]
    c[:, C_MB:C_MB + P] = i[:, None] >= i[None, :]
    tok = np.arange(2 * P)
    pos = np.stack([tok // 64, tok % 64]).astype(np.float32)
    freqs = (np.float32(10000.0) ** (-np.arange(32, dtype=np.float32) / np.float32(32))).astype(np.float32)
    ang = pos[:, :, None] * freqs
    cos, sin = np.cos(ang), np.sin(ang)
    for t in range(2):
        for a in range(2):
            for y in range(2):
                o = P * t + 64 * a + 32 * y
                c[:, C_COS + o:C_COS + o + 32] = cos[a, t * P:(t + 1) * P]
                c[:, C_SIN + o:C_SIN + o + 32] = sin[a, t * P:(t + 1) * P] * (-1 if y == 0 else 1)
    for j in range(4):
        c[32 * j, C_SEL2] = 1
        c[32 * j + 1, C_SEL2 + 1] = 1
        c[32 * j:32 * j + 20, C_SEL20:C_SEL20 + 20] = np.eye(20)
    c[:, C_IOTA4:C_IOTA4 + 4] = np.arange(4)
    c[:, C_POS] = i + 1
    c[:, C_POS + 1] = P - i
    c[:, C_POS + 2] = P - 1 - i
    c[:, C_POS + 3] = i
    c[:, C_EPS] = EPS
    return c


def kernel(**inputs):
    import numpy as _np
    import concourse.bacc as _bacc
    from concourse import mybir as _mybir
    from concourse.bass_utils import run_bass_kernel_spmd as _run

    a = {k: _np.asarray(v) for k, v in inputs.items()}

    def chunks(v):
        return v.reshape(-1, P).T

    rows = [chunks(a["mod_b0"]), chunks(a["mod_b1"])]
    rows += [chunks(a[n]) for n in ("norm_mix_g0", "norm_ffn_g0", "norm_mix_g1", "norm_ffn_g1",
                                    "conv_b0", "conv_norm_g0", "conv_norm_b0")]
    rows.append(a["conv_w0"].reshape(TAPS, CB, P).transpose(2, 1, 0).reshape(P, CB * TAPS))
    rows.append(_np.stack([a["c_ctx"], a["c"][0]]).reshape(2, KD, P).transpose(2, 1, 0).reshape(P, 2 * KD))
    for l in range(2):
        w = _np.concatenate([a[f"moe_grp_w{l}"], a[f"moe_rtr_w{l}"].transpose(1, 0, 2).reshape(D, NE)], axis=1)
        rows.append(w.reshape(KD, P, 20).transpose(1, 0, 2).reshape(P, KD * 20))
    flat = [_np.concatenate([a[f"moe_grp_b{l}"], a[f"moe_rtr_b{l}"].reshape(-1)]) for l in range(2)]
    flat += [a["ret_decay_fwd1"], a["ret_decay_bwd1"], a["q_norm_g0"], a["k_norm_g0"]]
    rows += [_np.broadcast_to(v, (P, v.size)) for v in flat]

    nc = _bacc.Bacc("TRN2", target_bir_lowering=False, num_devices=1)
    arrays = {}

    def given(name, v):
        arrays[name] = _np.ascontiguousarray(v)
        return nc.dram_tensor(name, v.shape, _mybir.dt.from_np(v.dtype), kind="ExternalInput").ap()

    def made(name, shape):
        return nc.dram_tensor(name, shape, _mybir.dt.from_np(_np.dtype("float32")), kind="ExternalOutput").ap()

    xs = _np.concatenate([a["x_prompt"][0], a["x_sample"][0]])
    args = [given("x_in", xs), given("cst", shape_constants()), given("par", _np.concatenate(rows, axis=1)),
            given("fgain", _np.broadcast_to(a["final_norm_g"], (P, D))),
            given("cache_k", a["cache_k0"][0]), given("cache_v", a["cache_v0"][0]),
            [given("st_f", a["state_ret_fwd1"][0]), given("st_b", a["state_ret_bwd1"][0])]]
    for n in ("mod_w", "in_w", "out_w", "moe_w_gate", "moe_w_up", "moe_w_down"):
        args.append([given(f"{n}{l}", a[f"{n}{l}"]) for l in range(2)])
    args += [made("y_out", (NT, D)), made("new_k", (KH, P, HD)), made("new_v", (KH, P, HD)),
             [made("new_st_f", (RH, DK, DV)), made("new_st_b", (RH, DK, DV))]]
    backbone_kernel(nc, *args)
    r = _run(nc, [arrays], core_ids=[0]).results[0]
    y = r["y_out"]
    return (y[None, 0:P], y[None, P:NT], r["new_k"][None], r["new_v"][None], r["new_st_f"][None], r["new_st_b"][None])
```
